# Optimizing a Trainium2 kernel written in Bass

```python
import math
import numpy as np
import jax
import jax.numpy as jnp
from jax import lax

D_MODEL = 1024
BATCH = 1
SEQ = 1024
DEPTH = 2
DEC_BATCH = 8
DEC_SEQ = 1
PAST_LEN = 1024
PAGE_SIZE = 128

N_A_LAYERS = DEPTH // 2
N_B_LAYERS = DEPTH - N_A_LAYERS
MIX_W = 3 * D_MODEL // 4
MEM_W = D_MODEL - MIX_W
HEAD_DIM = 64
MEM_HEADS = MEM_W // HEAD_DIM
MEM_TOKENS = 256
MLSTM_HEADS = 4
MLSTM_DH = MIX_W // MLSTM_HEADS
MLSTM_CHUNK = 64
NSA_HEADS = MIX_W // HEAD_DIM
NSA_KV_HEADS = 2
NSA_GROUP = NSA_HEADS // NSA_KV_HEADS
CMP_LEN = 32
CMP_STRIDE = 16
CMP_HIDDEN = 128
SLC_BLOCK = 64
N_SELECT = 8
WINDOW = 512
WIN_QBLOCK = 128
SLC_QBLOCK = 64
REL_BUCKETS = 32
REL_MAX_EXACT = 16
REL_MAX_DIST = 128
D_FF = -(-(8 * D_MODEL) // (3 * 256)) * 256
A_COLS = 4 * MIX_W + 2 * MLSTM_HEADS + MEM_W
B_COLS = MIX_W + 3 * NSA_HEADS + MEM_W
KV_COLS = 3 * 2 * NSA_KV_HEADS * HEAD_DIM
EPS = 1e-6
NEG = -1e30
FORCED = 1e6

kernel_name = 'yoco_mlstm_nsa_decode_step'

def rmsnorm(x, g):
    xf = x.astype(jnp.float32)
    y = xf * lax.rsqrt(jnp.mean(xf * xf, axis=-1, keepdims=True) + EPS)
    return (y * g.astype(jnp.float32)).astype(x.dtype)

def masked_softmax(s, mask):
    p = jax.nn.softmax(jnp.where(mask, s, NEG), axis=-1)
    return jnp.where(mask, p, 0.0)

def rel_bucket(dist):
    d = jnp.maximum(dist, 0)
    ratio = jnp.maximum(d, REL_MAX_EXACT).astype(jnp.float32) / REL_MAX_EXACT
    large = REL_MAX_EXACT + (jnp.log(ratio) / math.log(REL_MAX_DIST / REL_MAX_EXACT)
                             * (REL_BUCKETS - REL_MAX_EXACT)).astype(jnp.int32)
    return jnp.where(d < REL_MAX_EXACT, d, jnp.minimum(large, REL_BUCKETS - 1))

def swiglu(h, w_gu, w_down):
    gu = h @ w_gu
    return (jax.nn.silu(gu[..., :D_FF]) * gu[..., D_FF:]) @ w_down

def mem_kv_rows(mem, w, g_k):
    b, m, _ = mem.shape
    kv = (mem @ w).reshape(b, m, 2, MEM_HEADS, HEAD_DIM)
    return jnp.stack([rmsnorm(kv[:, :, 0], g_k), kv[:, :, 1]], axis=2)

def mem_attn(pm, mkv, g_q):
    b, s, _ = pm.shape
    q = rmsnorm(pm.reshape(b, s, MEM_HEADS, HEAD_DIM), g_q)
    sc = jnp.einsum('bshd,bmhd->bhsm', q, mkv[:, :, 0], preferred_element_type=jnp.float32) * HEAD_DIM ** -0.5
    p = jax.nn.softmax(sc, axis=-1)
    o = jnp.einsum('bhsm,bmhd->bshd', p.astype(mkv.dtype), mkv[:, :, 1])
    return o.reshape(b, s, MEM_W).astype(pm.dtype)

def mlstm_chunkwise(q, k, v, i_pre, logf, c0, n0, m0):
    b, s, h, d = q.shape
    L = MLSTM_CHUNK if s % MLSTM_CHUNK == 0 else s
    nc = s // L

    def chunks(a):
        return jnp.swapaxes(a.reshape(b, nc, L, *a.shape[2:]), 0, 1)

    causal = jnp.tril(jnp.ones((L, L), dtype=bool))

    def step(carry, xs):
        c, n, m = carry
        qc, kc, vc, ic, fc = xs
        bcum = jnp.swapaxes(jnp.cumsum(fc, axis=1), 1, 2)
        ig = jnp.swapaxes(ic, 1, 2)
        log_d = jnp.where(causal, bcum[..., :, None] - bcum[..., None, :] + ig[..., None, :], -jnp.inf)
        log_inter = bcum + m[..., None]
        m_t = jnp.maximum(jnp.max(log_d, axis=-1), log_inter)
        w_intra = jnp.exp(log_d - m_t[..., None])
        w_inter = jnp.exp(log_inter - m_t)
        sc = jnp.einsum('bthd,bshd->bhts', qc, kc) * w_intra
        num = jnp.einsum('bhts,bshd->bhtd', sc, vc) + w_inter[..., None] * jnp.einsum('bthd,bhde->bhte', qc, c)
        den = jnp.sum(sc, axis=-1) + w_inter * jnp.einsum('bthd,bhd->bht', qc, n)
        hh = num / jnp.maximum(jnp.abs(den), jnp.exp(-m_t))[..., None]
        g = bcum[..., -1]
        m_new = m_t[..., -1]
        w_s = jnp.exp(g[..., None] - bcum + ig - m_new[..., None])
        decay = jnp.exp(g + m - m_new)
        c_new = decay[..., None, None] * c + jnp.einsum('bhs,bshd,bshe->bhde', w_s, kc, vc)
        n_new = decay[..., None] * n + jnp.einsum('bhs,bshd->bhd', w_s, kc)
        return (c_new, n_new, m_new), jnp.swapaxes(hh, 1, 2)

    (c, n, m), hs = lax.scan(step, (c0, n0, m0), tuple(chunks(a) for a in (q, k, v, i_pre, logf)))
    return jnp.swapaxes(hs, 0, 1).reshape(b, s, h, d), (c, n, m)

def mlstm_mixer(p, state, b_if, g_hnorm):
    b, s, _ = p.shape
    f32 = jnp.float32

    def heads(a):
        return a.reshape(b, s, MLSTM_HEADS, MLSTM_DH).astype(f32)

    q = heads(p[..., :MIX_W])
    k = heads(p[..., MIX_W:2 * MIX_W]) * MLSTM_DH ** -0.5
    v = heads(p[..., 2 * MIX_W:3 * MIX_W])
    o = p[..., 3 * MIX_W:4 * MIX_W].astype(f32)
    gates = p[..., 4 * MIX_W:4 * MIX_W + 2 * MLSTM_HEADS].astype(f32) + b_if.astype(f32)
    i_pre = gates[..., :MLSTM_HEADS]
    logf = jax.nn.log_sigmoid(gates[..., MLSTM_HEADS:])
    c0, n0, m0 = (a.astype(f32) for a in state)
    h, new_state = mlstm_chunkwise(q, k, v, i_pre, logf, c0, n0, m0)
    h = rmsnorm(h, g_hnorm).reshape(b, s, MIX_W)
    return (jax.nn.sigmoid(o) * h).astype(p.dtype), new_state

def kv_rows(x, g_kv, w_kv, g_k_slc, g_k_win):
    b, s, _ = x.shape
    kv = (rmsnorm(x, g_kv) @ w_kv).reshape(b, s, 3, 2, NSA_KV_HEADS, HEAD_DIM)
    cmp = kv[:, :, 0]
    slc = jnp.stack([rmsnorm(kv[:, :, 1, 0], g_k_slc), kv[:, :, 1, 1]], axis=2)
    win = jnp.stack([rmsnorm(kv[:, :, 2, 0], g_k_win), kv[:, :, 2, 1]], axis=2)
    return cmp, slc, win

def compress(cmp_kv, w1, b1, w2, b2, pos_enc, g_k_cmp):
    b, t = cmp_kv.shape[:2]
    r_n = CMP_LEN // CMP_STRIDE
    nc = (t - CMP_LEN) // CMP_STRIDE + 1
    nseg = nc + r_n - 1
    seg = cmp_kv[:, :nseg * CMP_STRIDE].reshape(b, nseg, CMP_STRIDE, 2, NSA_KV_HEADS, HEAD_DIM)
    w1r = w1.reshape(2, r_n, CMP_STRIDE, HEAD_DIM, CMP_HIDDEN)
    pe = jnp.einsum('pcd,cpdh->ch', pos_enc, w1)
    pre = (b1 + pe)[None, None, :, None, :]
    for r in range(r_n):
        pre = pre + jnp.einsum('bnucgd,cudh->bncgh', seg[:, r:r + nc], w1r[:, r])
    out = jnp.einsum('bncgh,chd->bncgd', jax.nn.gelu(pre), w2) + b2[None, None, :, None, :]
    ck = rmsnorm(out[:, :, 0], g_k_cmp)
    cv = out[:, :, 1]
    c_end = jnp.arange(nc) * CMP_STRIDE + CMP_LEN - 1
    return ck, cv, c_end

def cmp_to_slc_matrix(n_cmp, n_slc):
    c0 = np.arange(n_cmp)[:, None] * CMP_STRIDE
    s0 = np.arange(n_slc)[None, :] * SLC_BLOCK
    ov = np.clip(np.minimum(c0 + CMP_LEN, s0 + SLC_BLOCK) - np.maximum(c0, s0), 0, None)
    return jnp.asarray(ov / CMP_STRIDE, dtype=jnp.float32)

def cmp_branch(q, qpos, ck, cv, c_end, table):
    sc = jnp.einsum('bsgzd,bngd->bsgzn', q, ck, preferred_element_type=jnp.float32) * HEAD_DIM ** -0.5
    dist = qpos[:, None] - c_end[None, :]
    bias = jnp.transpose(table[rel_bucket(dist)], (0, 2, 3, 1))
    p = masked_softmax(sc + bias[None], (dist >= 0)[:, None, None, :])
    o = jnp.einsum('bsgzn,bngd->bsgzd', p.astype(cv.dtype), cv)
    return o, p

def select_blocks(p_cmp, qpos, n_slc):
    imp = jnp.einsum('bsgzn,nj->bsgj', p_cmp, cmp_to_slc_matrix(p_cmp.shape[-1], n_slc))
    j = jnp.arange(n_slc)
    cur = (qpos // SLC_BLOCK)[:, None]
    valid = j <= cur
    forced = (j == 0) | (j == cur) | (j == cur - 1)
    score = jnp.where(forced[None, :, None], FORCED, jnp.where(valid[None, :, None], imp, -1.0))
    _, idx = lax.top_k(score, min(N_SELECT, n_slc))
    return idx

def slc_branch(q, qpos, idx, fetch, table):
    b, s = q.shape[:2]
    qb = SLC_QBLOCK if s % SLC_QBLOCK == 0 else s
    nb = s // qb
    g_i = jnp.arange(NSA_KV_HEADS)[None, None, :, None]

    def blk(args):
        qx, px, ix = args
        tok = (ix[..., None] * SLC_BLOCK + jnp.arange(SLC_BLOCK)).reshape(b, qb, NSA_KV_HEADS, -1)
        kx, vx = fetch(tok)
        sc = jnp.einsum('bsgzd,bsgjd->bsgzj', qx, kx, preferred_element_type=jnp.float32) * HEAD_DIM ** -0.5
        dist = px[None, :, None, None] - tok
        bias = jnp.swapaxes(table[rel_bucket(dist), g_i], -1, -2)
        p = masked_softmax(sc + bias, (dist >= 0)[:, :, :, None, :])
        return jnp.einsum('bsgzj,bsgjd->bsgzd', p.astype(vx.dtype), vx)

    qs = jnp.swapaxes(q.reshape(b, nb, qb, NSA_KV_HEADS, NSA_GROUP, HEAD_DIM), 0, 1)
    ids = jnp.swapaxes(idx.reshape(b, nb, qb, NSA_KV_HEADS, idx.shape[-1]), 0, 1)
    out = lax.map(blk, (qs, qpos.reshape(nb, qb), ids))
    return jnp.swapaxes(out, 0, 1).reshape(b, s, NSA_KV_HEADS, NSA_GROUP, HEAD_DIM)

def win_branch(q, q_pos0, wkv, wpos0, table):
    b, s = q.shape[:2]
    qb = WIN_QBLOCK if s % WIN_QBLOCK == 0 else s
    nb = s // qb
    lk = WINDOW + qb
    wpad = jnp.pad(wkv, ((0, 0), (WINDOW, 0), (0, 0), (0, 0), (0, 0)))
    starts = q_pos0 + jnp.arange(nb) * qb
    offs = jnp.arange(lk)
    kidx = starts[:, None] - wpos0 + offs[None, :]
    kpos = starts[:, None] - WINDOW + offs[None, :]

    def blk(args):
        qx, px, ki, kp = args
        kv = jnp.take(wpad, ki, axis=1)
        sc = jnp.einsum('bigzd,bjgd->bgzij', qx, kv[:, :, 0], preferred_element_type=jnp.float32) * HEAD_DIM ** -0.5
        dist = px[:, None] - kp[None, :]
        bias = jnp.transpose(table[rel_bucket(dist)], (2, 3, 0, 1))
        mask = (dist >= 0) & (dist < WINDOW) & (kp >= wpos0)[None, :]
        p = masked_softmax(sc + bias[None], mask)
        return jnp.einsum('bgzij,bjgd->bigzd', p.astype(kv.dtype), kv[:, :, 1])

    qs = jnp.swapaxes(q.reshape(b, nb, qb, NSA_KV_HEADS, NSA_GROUP, HEAD_DIM), 0, 1)
    qpos = (q_pos0 + jnp.arange(s)).reshape(nb, qb)
    out = lax.map(blk, (qs, qpos, kidx, kpos))
    return jnp.swapaxes(out, 0, 1).reshape(b, s, NSA_KV_HEADS, NSA_GROUP, HEAD_DIM)

def nsa_mixer(p, q_pos0, ctx, g_q, b_gate, rel_table):
    b, s, _ = p.shape
    q = rmsnorm(p[..., :MIX_W].reshape(b, s, NSA_HEADS, HEAD_DIM), g_q)
    q = q.reshape(b, s, NSA_KV_HEADS, NSA_GROUP, HEAD_DIM)
    gates = jax.nn.sigmoid(p[..., MIX_W:MIX_W + 3 * NSA_HEADS].astype(jnp.float32) + b_gate.astype(jnp.float32))
    gates = gates.reshape(b, s, 3, NSA_KV_HEADS, NSA_GROUP, 1)
    qpos = q_pos0 + jnp.arange(s)
    table = rel_table.astype(jnp.float32).reshape(REL_BUCKETS, NSA_KV_HEADS, NSA_GROUP)
    o_cmp, p_cmp = cmp_branch(q, qpos, ctx['ck'], ctx['cv'], ctx['c_end'], table)
    idx = select_blocks(p_cmp, qpos, ctx['n_slc'])
    o_slc = slc_branch(q, qpos, idx, ctx['fetch'], table)
    o_win = win_branch(q, q_pos0, ctx['wkv'], ctx['wpos0'], table)
    o = gates[:, :, 0] * o_cmp + gates[:, :, 1] * o_slc + gates[:, :, 2] * o_win
    return o.reshape(b, s, MIX_W).astype(p.dtype)

def run_trunk(x, q_pos0, mem_kv, init_states, build_ctx, prm):
    states = []
    ctx = None
    rows = None
    for l in range(DEPTH):
        h = rmsnorm(x, prm['g_mix'][l])
        if l < N_A_LAYERS:
            p = h @ prm['w_in_a'][l]
            mix, st = mlstm_mixer(p, init_states[l], prm['b_if'][l], prm['g_hnorm'][l])
            states.append(st)
        else:
            j = l - N_A_LAYERS
            p = h @ prm['w_in_b'][j]
            mix = nsa_mixer(p, q_pos0, ctx, prm['g_q'][j], prm['b_gate'][j], prm['rel_table'])
        mem_o = mem_attn(p[..., -MEM_W:], mem_kv[l], prm['g_mem_q'][l])
        x = x + jnp.concatenate([mix, mem_o], axis=-1) @ prm['w_out'][l]
        x = x + swiglu(rmsnorm(x, prm['g_ffn'][l]), prm['w_gu'][l], prm['w_down'][l])
        if l == N_A_LAYERS - 1:
            rows = kv_rows(x, prm['g_kv'], prm['w_kv'], prm['g_k_slc'], prm['g_k_win'])
            ctx = build_ctx(*rows)
    new_states = tuple(jnp.stack([st[i] for st in states]) for i in range(3))
    return x, new_states, rows

def setup_inputs(seed: int = 0) -> dict:
    key = jax.random.key(seed)
    keys = iter(jax.random.split(key, 48))

    def nrm(shape, scale=1.0):
        return jax.random.normal(next(keys), shape, jnp.float32) * scale

    def gain(shape):
        return 1.0 + nrm(shape, 0.02)

    n_pages = PAST_LEN // PAGE_SIZE
    n_pool = (DEC_BATCH * n_pages * 5 + 3) // 4
    wb = min(WINDOW, PAST_LEN)
    d_in = D_MODEL ** -0.5
    res = (2 * DEPTH) ** -0.5
    kvh, hd = NSA_KV_HEADS, HEAD_DIM
    page_table = jax.random.permutation(next(keys), n_pool)[:DEC_BATCH * n_pages].reshape(DEC_BATCH, n_pages).astype(jnp.int32)
    b_if = jnp.concatenate([nrm((N_A_LAYERS, MLSTM_HEADS), 0.1),
                            jnp.linspace(3.0, 6.0, MLSTM_HEADS, dtype=jnp.float32)[None, :] + nrm((N_A_LAYERS, MLSTM_HEADS), 0.1)], axis=-1)
    return {
        'x_prompt': nrm((BATCH, SEQ, D_MODEL)),
        'x_sample': nrm((DEC_BATCH, DEC_SEQ, D_MODEL)),
        'state_mlstm_c': nrm((N_A_LAYERS, DEC_BATCH, MLSTM_HEADS, MLSTM_DH, MLSTM_DH), 0.05),
        'state_mlstm_n': nrm((N_A_LAYERS, DEC_BATCH, MLSTM_HEADS, MLSTM_DH), 0.5),
        'state_mlstm_m': nrm((N_A_LAYERS, DEC_BATCH, MLSTM_HEADS), 1.0),
        'cache_mem_kv': nrm((DEPTH, DEC_BATCH, MEM_TOKENS, 2, MEM_HEADS, hd)),
        'cache_cmp_kv': nrm((n_pool, PAGE_SIZE, 2, kvh, hd)),
        'cache_slc_kv': nrm((n_pool, PAGE_SIZE, 2, kvh, hd)),
        'cache_win_kv': nrm((DEC_BATCH, wb, 2, kvh, hd)),
        'page_table': page_table,
        'mem_prompt': nrm((BATCH, MEM_TOKENS, D_MODEL)),
        'g_mix': gain((DEPTH, D_MODEL)),
        'w_in_a': nrm((N_A_LAYERS, D_MODEL, A_COLS), d_in),
        'b_if': b_if,
        'g_hnorm': gain((N_A_LAYERS, MLSTM_DH)),
        'w_in_b': nrm((N_B_LAYERS, D_MODEL, B_COLS), d_in),
        'g_q': gain((N_B_LAYERS, hd)),
        'b_gate': nrm((N_B_LAYERS, 3 * NSA_HEADS), 0.1),
        'rel_table': nrm((REL_BUCKETS, NSA_HEADS), 0.5),
        'g_kv': gain((D_MODEL,)),
        'w_kv': nrm((D_MODEL, KV_COLS), d_in),
        'g_k_slc': gain((hd,)),
        'g_k_win': gain((hd,)),
        'g_k_cmp': gain((hd,)),
        'cmp_pos': nrm((CMP_LEN, 2, hd), 0.1),
        'cmp_w1': nrm((2, CMP_LEN, hd, CMP_HIDDEN), (CMP_LEN * hd) ** -0.5),
        'cmp_b1': nrm((2, CMP_HIDDEN), 0.02),
        'cmp_w2': nrm((2, CMP_HIDDEN, hd), CMP_HIDDEN ** -0.5),
        'cmp_b2': nrm((2, hd), 0.02),
        'w_mem_kv': nrm((DEPTH, D_MODEL, 2 * MEM_W), d_in),
        'g_mem_k': gain((DEPTH, hd)),
        'g_mem_q': gain((DEPTH, hd)),
        'w_out': nrm((DEPTH, D_MODEL, D_MODEL), d_in * res),
        'g_ffn': gain((DEPTH, D_MODEL)),
        'w_gu': nrm((DEPTH, D_MODEL, 2 * D_FF), d_in),
        'w_down': nrm((DEPTH, D_FF, D_MODEL), D_FF ** -0.5 * res),
    }

def reference(x_prompt, x_sample, state_mlstm_c, state_mlstm_n, state_mlstm_m, cache_mem_kv,
              cache_cmp_kv, cache_slc_kv, cache_win_kv, page_table, mem_prompt,
              g_mix, w_in_a, b_if, g_hnorm, w_in_b, g_q, b_gate, rel_table, g_kv, w_kv,
              g_k_slc, g_k_win, g_k_cmp, cmp_pos, cmp_w1, cmp_b1, cmp_w2, cmp_b2,
              w_mem_kv, g_mem_k, g_mem_q, w_out, g_ffn, w_gu, w_down):
    prm = {'g_mix': g_mix, 'w_in_a': w_in_a, 'b_if': b_if, 'g_hnorm': g_hnorm, 'w_in_b': w_in_b,
           'g_q': g_q, 'b_gate': b_gate, 'rel_table': rel_table, 'g_kv': g_kv, 'w_kv': w_kv,
           'g_k_slc': g_k_slc, 'g_k_win': g_k_win, 'g_mem_q': g_mem_q, 'w_out': w_out,
           'g_ffn': g_ffn, 'w_gu': w_gu, 'w_down': w_down}
    g_i = jnp.arange(NSA_KV_HEADS)[None, None, :, None]

    b_p, s_p, _ = x_prompt.shape
    mem_kv_p = jnp.stack([mem_kv_rows(mem_prompt, w_mem_kv[l], g_mem_k[l]) for l in range(DEPTH)])
    init_p = [(jnp.zeros((b_p, MLSTM_HEADS, MLSTM_DH, MLSTM_DH), jnp.float32),
               jnp.zeros((b_p, MLSTM_HEADS, MLSTM_DH), jnp.float32),
               jnp.full((b_p, MLSTM_HEADS), NEG, jnp.float32)) for _ in range(N_A_LAYERS)]
    b_ip = jnp.arange(b_p)[:, None, None, None]

    def ctx_prompt(cmp_rows, slc_rows, win_rows):
        ck, cv, c_end = compress(cmp_rows, cmp_w1, cmp_b1, cmp_w2, cmp_b2, cmp_pos, g_k_cmp)

        def fetch(tok):
            kv = slc_rows[b_ip, jnp.minimum(tok, s_p - 1), :, g_i]
            return kv[..., 0, :], kv[..., 1, :]

        return {'ck': ck, 'cv': cv, 'c_end': c_end, 'n_slc': -(-s_p // SLC_BLOCK),
                'fetch': fetch, 'wkv': win_rows, 'wpos0': 0}

    y_p, st_p, rows_p = run_trunk(x_prompt, 0, mem_kv_p, init_p, ctx_prompt, prm)

    b_s, s_s, _ = x_sample.shape
    past = page_table.shape[1] * PAGE_SIZE
    wb = cache_win_kv.shape[1]
    init_s = [(state_mlstm_c[l], state_mlstm_n[l], state_mlstm_m[l]) for l in range(N_A_LAYERS)]
    b_is = jnp.arange(b_s)[:, None, None, None]

    def ctx_sample(cmp_new, slc_new, win_new):
        cmp_past = cache_cmp_kv[page_table].reshape(b_s, past, 2, NSA_KV_HEADS, HEAD_DIM)
        ck, cv, c_end = compress(jnp.concatenate([cmp_past, cmp_new], axis=1),
                                 cmp_w1, cmp_b1, cmp_w2, cmp_b2, cmp_pos, g_k_cmp)

        def fetch(tok):
            tp = jnp.minimum(tok, past - 1)
            phys = page_table[b_is, tp // PAGE_SIZE]
            kv_old = cache_slc_kv[phys, tp % PAGE_SIZE, :, g_i]
            kv_new = slc_new[b_is, jnp.clip(tok - past, 0, s_s - 1), :, g_i]
            kv = jnp.where((tok < past)[..., None, None], kv_old, kv_new)
            return kv[..., 0, :], kv[..., 1, :]

        return {'ck': ck, 'cv': cv, 'c_end': c_end, 'n_slc': -(-(past + s_s) // SLC_BLOCK),
                'fetch': fetch, 'wkv': jnp.concatenate([cache_win_kv, win_new], axis=1), 'wpos0': past - wb}

    y_s, st_s, rows_s = run_trunk(x_sample, past, cache_mem_kv, init_s, ctx_sample, prm)

    p_win = rows_p[2][:, s_p - min(WINDOW, s_p):]
    s_win = jnp.concatenate([cache_win_kv, rows_s[2]], axis=1)[:, -wb:]
    return (y_p, y_s, st_p[0], st_p[1], st_p[2], mem_kv_p, rows_p[0], rows_p[1], p_win,
            st_s[0], st_s[1], st_s[2], rows_s[0], rows_s[1], s_win)


_drawn_inputs = setup_inputs


def setup_inputs(seed=0):
    import zlib

    import numpy as np

    out = dict(_drawn_inputs(seed))
    spreads = {}
    factors = {'cache_slc_kv': 3.028,
     'g_hnorm': 8.0,
     'g_q': 21.446,
     'b_gate': 8.0,
     'rel_table': 2.977,
     'g_kv': 2.925,
     'g_k_slc': 19.867,
     'g_k_win': 15.629,
     'g_k_cmp': 8.0,
     'cmp_pos': 4.223,
     'cmp_b1': 8.0,
     'cmp_b2': 21.463,
     'g_mem_k': 3.925,
     'g_mem_q': 8.0,
     'g_ffn': 5.036}
    for name, (base, spread) in spreads.items():
        noise = np.random.default_rng([zlib.crc32(name.encode()), seed]).standard_normal(out[name].shape)
        drawn = base * np.exp(spread * noise) if base else spread * noise
        out[name] = jnp.asarray(drawn.astype(out[name].dtype))
    for name, factor in factors.items():
        out[name] = (out[name] * factor).astype(out[name].dtype)
    return out
```

```python
from contextlib import ExitStack

import concourse.bass as bass
from concourse import mybir
import numpy as np

F32 = mybir.dt.float32
F32R = mybir.dt.float32r
I32 = mybir.dt.int32
ALU = mybir.AluOpType
ACT = mybir.ActivationFunctionType
AX = mybir.AxisListType.X

P = 128
DM = 1024
SEQ = 1024
NB = 8
N = SEQ + NB
KC = DM // P
CH = N // 3
MIX = 768
HD = 64
MH = 4
DH = MIX // MH
MEM = 256
NH = 12
FF = 2816
FT = FF // P
FCUT = [0, 8, 15, 22]
EPS = 1e-6
NEG = -1e30
NT = SEQ // P
NCMP = 63

_C = {}


def constants():
    cols, at = [], 0

    def put(name, a):
        nonlocal at
        full = np.zeros((P, a.shape[1]), np.float32)
        full[:a.shape[0]] = a
        _C[name] = (at, a.shape[0], a.shape[1])
        cols.append(full)
        at += a.shape[1]

    put("ident", np.eye(P))
    put("ones", np.ones((P, P)))
    blk = np.zeros((P, P))
    blk[:64, :64] = blk[64:, 64:] = 1
    put("pairs", blk)
    cm = np.zeros((P, 512))
    cm[:, :P] = np.where(np.arange(P)[None, :] >= np.arange(P)[:, None], 0, NEG)
    put("causal", cm)
    sel = np.zeros((4, 4 * P))
    for h in range(4):
        sel[h, h * P:(h + 1) * P] = 1
    put("head_rows", sel)
    r64 = np.zeros((4, 4 * 65))
    for h in range(4):
        r64[h, h * 65 + 64] = 1
    put("head_row64", r64)
    put("eye8", np.eye(8))
    er = np.zeros((P, P))
    er[64] = DH * EPS
    hr = np.zeros((P, 2 * P))
    hr[:64, :P] = hr[64:, P:] = 1
    put("half_rows", hr)
    put("eps_row", er)
    return np.concatenate(cols, 1)


_C2 = {}
TINY = 1.1754944e-38


def constants2():
    cols, at = [], 0

    def put(name, a):
        nonlocal at
        full = np.zeros((P, a.shape[1]), np.float32)
        full[:a.shape[0]] = a
        _C2[name] = (at, a.shape[0], a.shape[1])
        cols.append(full)
        at += a.shape[1]

    def rules(q, n):
        cur, j = q[:, None] // 64, np.arange(n)[None, :]
        force = (j == 0) | (j == cur) | (j == cur - 1)
        ok = j <= cur
        return (ok & ~force).astype(np.float32), np.where(force, 1e6, np.where(ok, 0, -1)).astype(np.float32)

    vf = [rules(i * P + np.arange(P), 16) for i in range(NT)]
    put("valid", np.concatenate([v for v, _ in vf], 1))
    put("forced", np.concatenate([f for _, f in vf], 1))
    for name, n in (("before", 16), ("before_s", 17)):
        put(name, np.broadcast_to((np.arange(n)[None, :] < np.arange(n)[:, None]).reshape(1, -1), (P, n * n)))
    put("edge", np.where(np.arange(P)[None, :] <= np.arange(P)[:, None], NEG, 0))
    put("seen", (np.arange(P) >= 31).astype(np.float32)[:, None])
    R = NB * NH
    v, f = rules(np.full(R, SEQ), 17)
    put("valid_s", v)
    put("forced_s", f)
    row_b, row_h = np.arange(R) // NH, np.arange(R) % NH
    put("b_rows", (row_b[None, :] == np.arange(NB)[:, None]).astype(np.float32))
    put("row_b", (row_b[:, None] == np.arange(NB)[None, :]).astype(np.float32))
    put("h_pick", (np.arange(36)[None, :] % NH == row_h[:, None]).astype(np.float32))
    grp = row_b * 2 + row_h // 6
    put("groups", (grp[:, None] == grp[None, :]).astype(np.float32))
    return np.concatenate(cols, 1)


def one_hot(d):
    a = np.zeros((33, len(d)), np.float32)
    at = np.arange(len(d))
    a[bucket(d), at] += 1
    a[31] -= 1
    a[:, d < 0] = 0
    a[32, d < 0] = 1
    return a


def bucket(d):
    d = np.maximum(d, 0)
    ratio = np.maximum(d, 16).astype(np.float32) / np.float32(16)
    large = 16 + (np.log(ratio) / np.float32(np.log(8.0)) * np.float32(16)).astype(np.int32)
    return np.where(d < 16, d, np.minimum(large, 31))


def step(nc, A, O, stop=99):
    with ExitStack() as ctx:
        top = [(nc.sbuf_base + 63) // 64 * 64]

        def place(name, shape, dt=F32, at=None):
            size = 4 * int(np.prod(shape[1:]))
            where = top[0] if at is None else at
            if at is None:
                top[0] += (size + 63) // 64 * 64
            return nc.alloc_sbuf_tensor_at(name, list(shape), dt, offset=where)

        def sem(name):
            return ctx.enter_context(nc.semaphore(name))

        xT = place("xT", [P, KC, N])
        x_end = top[0]
        h_hi = place("h_hi", [P, KC, N], F32R)
        h_lo = place("h_lo", [P, KC, N], F32R)
        w_raw = place("w_raw", [P, 2, DM])
        w_hi_at = top[0]
        w_hi = place("w_hi", [P, 2, DM], F32R)
        w_lo = place("w_lo", [P, 2, DM], F32R)
        con = place("con", [P, A["con"].shape[1]])
        gain = place("gain", [P, A["gain"].shape[1]])
        mem_kT = place("mem_kT", [P, 2, 2, MEM])
        mem_v = place("mem_v", [P, 2, 2, 256])
        eps_c = place("eps_c", [P, 1])
        rows2 = place("rows2", [36, N])
        vsT = place("vsT", [P, 6, NB])
        arena = top[0]
        arena_end = nc.sbuf_usable_end
        mix = place("mix", [P, KC, N], at=arena)
        a2 = arena + 4 * KC * N
        kT = place("kT", [P, 6, N], at=a2)
        v_ext = place("v_ext", [P, NT, MH, DH + 1], at=a2 + 4 * 6 * N)
        aend = a2 + 4 * 6 * N + 4 * NT * MH * (DH + 1)
        pass
        hid_hi = place("hid_hi", [P, 8, N], F32R, at=arena)
        hid_lo = place("hid_lo", [P, 8, N], F32R, at=arena + 32 * N)
        f_silu = place("f_silu", [P, N], at=arena + 64 * N)
        f_t = place("f_t", [P, N], at=arena + 68 * N)
        assert arena + 72 * N <= arena_end
        n_a = [place("na_r", [P, N], at=arena), place("na_t", [P, 2, N], at=arena + 4 * N),
               place("na_acc", [P, N], at=arena + 12 * N)]
        n_b = [place("nb_r", [P, N], at=arena + 72 * N), place("nb_t", [P, 2, N], at=arena + 64 * N),
               place("nb_acc", [P, N], at=arena + 76 * N)]
        n_buf = [n_a, n_b, n_b, n_a, n_b]
        assert arena + 80 * N <= arena_end
        ps = ctx.enter_context(nc.psum_tensor("ps", [P, 8, 512], F32))

        def C(name, rows=P, lo=0, n=None):
            at, r, w = _C[name]
            return con[0:rows, at + lo:at + (w if n is None else lo + n)]

        def G(name, i=0, rows=P, p0=0):
            return gain[p0:p0 + rows, _G[name] + i:_G[name] + i + 1]

        con_in = sem("con_in")
        w_in = [sem("w_in0"), sem("w_in1")]
        w_hi_ready, w_lo_ready = sem("w_hi_ready"), sem("w_lo_ready")
        tile_done = sem("tile_done")
        tile_free = sem("tile_free")
        hid_ready = sem("hid_ready")
        fence_s = sem("fence")
        out_s = sem("out_s")
        outs = [0]

        def fence(eng, n):
            eng.drain()
            eng.sem_inc(fence_s, 1)
            eng.wait_ge(fence_s, 3 * n)

        segs, t = {}, 0

        def seg(name, n, kk, src, at):
            nonlocal t
            segs[name] = (t, n, kk, src, at)
            t += n
        seg("mem", 8, 8, "w_mem", 0)
        seg("a_v", 6, 8, "w_a", 0)
        seg("a_q", 6, 8, "w_a", 6)
        seg("a_m", 2, 8, "w_a", 12)
        seg("a_g", 1, 8, "w_a", 14)
        seg("a_k", 6, 8, "w_a", 15)
        seg("a_o", 6, 8, "w_a", 21)
        seg("out0", 8, 8, "w_o0", 0)

        def ffn_segs(l):
            at = 0
            for q in range(3):
                k0, k1 = FCUT[q], FCUT[q + 1]
                seg(f"gu{l}{q}", 2 * (k1 - k0), 8, f"w_gu{l}", 2 * k0)
                seg(f"dn{l}{q}", 8, k1 - k0, f"w_dn{l}{q}", 0)
        ffn_segs(0)
        seg("kv", 6, 8, "w_kv", 0)
        seg("b_q", 9, 8, "w_b", 0)
        seg("out1", 8, 8, "w_o1", 0)
        ffn_segs(1)
        order = list(segs)

        def tiles(eng, name, body, peel=False):
            T0, n = segs[name][:2]
            if n >= 6 and T0 > 1:
                pairs = (n - 1) // 2
                if peel:
                    for i in range(2):
                        body(i, T0 + i, (T0 + i) % 2, 0)
                with eng.Fori(1 if peel else 0, pairs) as j:
                    for b in range(2):
                        body(j * 2 + b, j * 2 + (T0 + b), (T0 + b) % 2, j)
                rest = range(2 * pairs, n)
            else:
                rest = range(n)
            for i in rest:
                body(i, T0 + i, (T0 + i) % 2, i // 2)

        def load_seg(sp, name):
            _, _, kk, src, at = segs[name]

            def body(i, T, slot, j):
                if not (isinstance(T, int) and T < 2):
                    sp.wait_ge(w_lo_ready, T - 1)
                sp.dma_start(w_raw[:, slot, 0:kk * P], A[src][i + at]).then_inc(w_in[slot], 16)
            tiles(sp, name, body)

        def kk_after(name, i):
            n, kk = segs[name][1:3]
            if isinstance(i, int) and i == n - 1:
                k = order.index(name) + 1
                return segs[order[k]][2] if k < len(order) else None
            return kk

        def split_hi(act, T, slot, kk):
            act.wait_ge(w_in[slot], T * 8 + (16 - 8 * slot))
            if not (isinstance(T, int) and T < 2):
                act.wait_ge(tile_done, T - 1)
            act.activation(w_hi[:, slot, 0:kk * P], w_raw[:, slot, 0:kk * P], ACT.Copy).then_inc(w_hi_ready, 1)

        def split_lo(dve, T, slot, kk):
            if not (isinstance(T, int) and T < 2):
                dve.wait_ge(tile_done, T - 1)
            dve.wait_ge(w_hi_ready, T + 1)
            dve.tensor_tensor(w_lo[:, slot, 0:kk * P], w_raw[:, slot, 0:kk * P],
                              w_hi[:, slot, 0:kk * P].bitcast(F32), ALU.subtract).then_inc(w_lo_ready, 1)

        def seg_act(act, name, evac=None, first=False, chain=True):
            T0, n, kk = segs[name][:3]
            if first:
                split_hi(act, T0, T0 % 2, kk)

            def body(i, T, slot, j):
                nk = kk_after(name, i)
                if nk and (chain or not (isinstance(i, int) and i == n - 1)):
                    split_hi(act, T + 1, 1 - slot, nk)
                if evac:
                    evac(i, T, slot, j)
            tiles(act, name, body)

        def seg_dve(dve, name, evac=None, first=False, chain=True):
            T0, n, kk = segs[name][:3]
            if first:
                split_lo(dve, T0, T0 % 2, kk)

            def body(i, T, slot, j):
                nk = kk_after(name, i)
                if nk and (chain or not (isinstance(i, int) and i == n - 1)):
                    split_lo(dve, T + 1, 1 - slot, nk)
                if evac:
                    evac(i, T, slot, j)
            tiles(dve, name, body)

        def seg_pe(pe, name, a_hi=h_hi, a_lo=h_lo, cut=CH, nch=3, ready=None):
            T0, n, kk = segs[name][:3]

            def body(i, T, slot, j):
                pe.wait_ge(w_hi_ready, T + 1)
                pe.wait_ge(w_lo_ready, T + 1)
                if not (isinstance(T, int) and T < 2):
                    pe.wait_ge(tile_free, T - 1)
                for k in range(kk):
                    if ready and isinstance(i, int) and i == 0:
                        pe.wait_ge(*ready(k))
                    for w, a in ((w_hi, a_hi), (w_hi, a_lo), (w_lo, a_hi)):
                        for c in range(nch):
                            mm = pe.matmul(ps[:, 3 * slot + c, 0:cut], w[:, slot, k * P:(k + 1) * P],
                                           a[:, k, c * cut:(c + 1) * cut],
                                           start=(k == 0 and w is w_hi and a is a_hi),
                                           stop=(k == kk - 1 and w is w_lo))
                mm.then_inc(tile_done, 1)
            tiles(pe, name, body, peel=ready is not None)

        def acc(slot):
            return ps[:, 3 * slot:3 * slot + 3, 0:CH]

        def three(ap):
            return ap.rearrange("p (c t) -> p c t", c=3)

        n_sq, n_add, n_ss, n_rt, n_h, n_hi, n_lo, n_z = (
            sem(x) for x in ("n_sq", "n_add", "n_ss", "n_rt", "n_h", "n_hi", "n_lo", "n_z"))

        def square_act(act, k, c, b):
            if not (isinstance(c, int) and c < 2):
                act.wait_ge(n_add, c + (8 * k - 1))
            act.activation(n_buf[k][1][:, b, :], xT[:, c, :], ACT.Square).then_inc(n_sq, 1)

        def square_dve(dve, k, c, b):
            acc_ = n_buf[k][2]
            dve.drain()
            dve.wait_ge(n_sq, c + (8 * k + 1))
            dve.tensor_tensor(acc_[:, :], acc_[:, :], n_buf[k][1][:, b, :], ALU.add).then_inc(n_add, 1)

        def norm_act(act, k, squares=False, first=None):
            if first:
                T0, _, kk = segs[first][:3]
                split_hi(act, T0, T0 % 2, kk)
            if squares:
                for c in range(KC):
                    square_act(act, k, c, c % 2)
            n_r, n_t, _ = n_buf[k]
            act.wait_ge(n_ss, k + 1)
            act.activation(three(n_r[:, :]), acc(0), ACT.Sqrt, bias=eps_c[:, 0:1], scale=1.0 / DM).then_inc(n_rt, 1)
            for c in range(KC):
                act.wait_ge(n_h, 8 * k + c + 1)
                act.activation(h_hi[:, c, :], n_t[:, c % 2, :], ACT.Copy).then_inc(n_hi, 1)

        def norm_dve(dve, k, g, squares=False, first=None):
            n_r, n_t, acc_ = n_buf[k]
            if first:
                T0, _, kk = segs[first][:3]
                split_lo(dve, T0, T0 % 2, kk)
            if squares:
                dve.memset(acc_[:, :], 0.0)
                for c in range(KC):
                    square_dve(dve, k, c, c % 2)
            dve.wait_ge(n_rt, k + 1)
            dve.reciprocal(n_r[:, :], n_r[:, :])
            dve.drain()

            def scaled(c):
                dve.scalar_tensor_tensor(out=n_t[:, c % 2, :], in0=xT[:, c, :], scalar=G(g, c), in1=n_r[:, :],
                                         op0=ALU.mult, op1=ALU.mult).then_inc(n_h, 1)
            scaled(0)
            for c in range(KC):
                if c + 1 < KC:
                    if c >= 1:
                        dve.wait_ge(n_hi, 8 * k + c)
                        dve.drain()
                    scaled(c + 1)
                dve.wait_ge(n_hi, 8 * k + c + 1)
                dve.drain()
                dve.tensor_tensor(h_lo[:, c, :], n_t[:, c % 2, :], h_hi[:, c, :].bitcast(F32),
                                  ALU.subtract).then_inc(n_lo, 1)

        def norm_pe(pe, k):
            pe.wait_ge(n_add, 8 * (k + 1))
            for c in range(3):
                mm = pe.matmul(ps[:, c, 0:CH], C("ones"), n_buf[k][2][:, c * CH:(c + 1) * CH], start=True, stop=True)
            mm.then_inc(n_ss, 1)

        def normed(k):
            return lambda c: (n_lo, 8 * k + c + 1)

        s_hi = sem("s_hi")
        s_n = [0]

        def split_act(act, base, src, n):
            for c in range(KC):
                act.activation(h_hi[:, c, 0:n], src[:, c, 0:n], ACT.Copy).then_inc(s_hi, 1)

        def split_dve(dve, base, src, n):
            for c in range(KC):
                dve.wait_ge(s_hi, base + c + 1)
                dve.tensor_tensor(h_lo[:, c, 0:n], src[:, c, 0:n], h_hi[:, c, 0:n].bitcast(F32), ALU.subtract)

        ld = sem("ld")
        m_ev, m_tr, m_tv = sem("m_ev"), sem("m_tr"), sem("m_tv")
        hn_sq, hn_ss, hn_rt, hn_o = sem("hn_sq"), sem("hn_ss"), sem("hn_rt"), sem("hn_o")
        hn_base = {"pe": 0, "act": 0, "dve": 0}

        def hnorm_act(act, src, n, cut, ncut, sq, rt):
            b = hn_base["act"]
            hn_base["act"] += n

            def root(t):
                act.wait_ge(hn_ss, b + t + 1)
                act.activation(rt[:, t % 2, 0:cut * ncut].rearrange("p (c t) -> p c t", c=ncut),
                               ps[:, 3 * (t % 2):3 * (t % 2) + ncut, 0:cut], ACT.Sqrt, bias=eps_c[:, 0:1],
                               scale=1.0 / HD).then_inc(hn_rt, 1)
            for t in range(n):
                if t >= 2:
                    act.wait_ge(hn_o, b + t - 1)
                act.activation(sq[:, t % 2, 0:cut * ncut], src(t), ACT.Square).then_inc(hn_sq, 1)
                if t >= 1:
                    root(t - 1)
            root(n - 1)

        def hnorm_pe(pe, n, cut, ncut, sq):
            b = hn_base["pe"]
            hn_base["pe"] += n
            for t in range(n):
                pe.wait_ge(hn_sq, b + t + 1)
                for c in range(ncut):
                    mm = pe.matmul(ps[:, 3 * (t % 2) + c, 0:cut], C("pairs"), sq[:, t % 2, c * cut:(c + 1) * cut],
                                   start=True, stop=True)
                mm.then_inc(hn_ss, 1)

        def hnorm_dve(dve, src, dst, n, w, g, rt):
            b = hn_base["dve"]
            hn_base["dve"] += n
            for t in range(n):
                dve.wait_ge(hn_rt, b + t + 1)
                dve.reciprocal(rt[:, t % 2, 0:w], rt[:, t % 2, 0:w])
                dve.drain()
                dve.scalar_tensor_tensor(out=dst(t), in0=src(t), scalar=g(t), in1=rt[:, t % 2, 0:w],
                                         op0=ALU.mult, op1=ALU.mult).then_inc(hn_o, 1)

        hm_sq = place("hm_sq", [P, 2, 256], at=a2)
        hm_rt = place("hm_rt", [P, 2, 256], at=a2 + 2048)

        def mem_k(t):
            l, pair = t // 2, t % 2
            return mix[:, 4 * l + pair, 256:512]

        def mem_sp(sp):
            sp.dma_start(con[:, :], A["con"]).then_inc(con_in, 16)
            sp.dma_start(gain[:, :], A["gain"]).then_inc(con_in, 16)
            sp.dma_start(mix[:, :, 0:256], A["memT"]).then_inc(ld, 16)
            load_seg(sp, "mem")
            sp.dma_start(xT[:, :, :], A["xT"]).then_inc(ld, 16)

        def mem_act(act):
            act.wait_ge(ld, 16)
            split_act(act, 0, mix, 256)

            def evac(i, T, slot, j):
                act.wait_ge(tile_done, T + 1)
                act.activation(mix[:, i, 256:512], ps[:, 3 * slot, 0:256], ACT.Copy).then_inc(tile_free, 1)
            seg_act(act, "mem", evac, first=True)
            act.drain()
            act.sem_inc(m_ev, 1)
            for l in range(2):
                for pair in range(2):
                    act.wait_ge(m_tr, 2 * l + pair + 1)
                    act.activation(mem_v[:, l, :, pair * P:(pair + 1) * P],
                                   ps[:, 6, 0:256].rearrange("p (m d) -> p m d", m=2), ACT.Copy).then_inc(m_tv, 1)
            hnorm_act(act, mem_k, 4, 256, 1, hm_sq, hm_rt)
            act.wait_ge(hn_o, 4)
            for t in range(8):
                l, j = t // 4, t % 4
                act.dma_start(O["o_mem"][t], mem_kT[:, l, j, :] if j < 2 else mix[:, t, 256:512]).then_inc(out_s, 16)
            outs[0] += 8
            act.wait_ge(out_s, 16 * outs[0])

        def mem_dve(dve):
            dve.memset(eps_c[:, :], EPS)
            split_dve(dve, 0, mix, 256)
            dve.drain()
            dve.sem_inc(s_lo, 1)
            seg_dve(dve, "mem", None, first=True)
            hnorm_dve(dve, mem_k, lambda t: mem_kT[:, t // 2, t % 2, :], 4, 256,
                      lambda t: G("g_mem_k", t // 2), hm_rt)

        def mem_pe(pe):
            pe.wait_ge(con_in, 32)
            pe.wait_ge(s_lo, 1)
            seg_pe(pe, "mem", cut=256, nch=1)
            pe.wait_ge(m_ev, 1)
            for l in range(2):
                for pair in range(2):
                    if l or pair:
                        pe.wait_ge(m_tv, 2 * l + pair)
                    for m in range(2):
                        mm = pe.transpose(ps[:, 6, m * P:(m + 1) * P],
                                          mix[:, 4 * l + 2 + pair, 256 + m * P:256 + (m + 1) * P], C("ident"))
                    mm.then_inc(m_tr, 1)
            hnorm_pe(pe, 4, 256, 1, hm_sq)
        s_lo = sem("s_lo")

        wk_at = w_hi_at - 8 * DM
        rows0 = place("rows0", [36, N], at=wk_at)
        rows1 = place("rows1", [36, N], at=wk_at + 4 * N)
        a_ev = sem("a_ev")
        v_tr, v_cp = sem("v_tr"), sem("v_cp")

        def proj_a_act(act):
            def to(buf, off=0, scale=None):
                def evac(i, T, slot, j):
                    act.wait_ge(tile_done, T + 1)
                    if scale is None:
                        act.activation(three(buf[:, i + off, :]), acc(slot), ACT.Copy).then_inc(tile_free, 1)
                    else:
                        act.activation(three(buf[:, i + off, :]), acc(slot), ACT.Copy, scale=scale).then_inc(tile_free, 1)
                return evac
            seg_act(act, "a_v", to(kT))
            act.drain()
            act.activation(vsT[:, :, :], kT[:, :, SEQ:N], ACT.Copy).then_inc(a_ev, 1)
            seg_act(act, "a_q", to(mix))
            seg_act(act, "a_m", to(mix, 6))

            def gates(i, T, slot, j):
                act.wait_ge(tile_done, T + 1)
                act.activation(three(rows2[:, :]), ps[0:36, 3 * slot:3 * slot + 3, 0:CH], ACT.Identity,
                               bias=G("b_if", 0, 36)).then_inc(tile_free, 1)
            seg_act(act, "a_g", gates)
            act.wait_ge(v_tr, 2 * 6)
            seg_act(act, "a_k", to(kT, 0, DH ** -0.5), chain=False)

        def v_heads(t):
            j, r = t // 3, t % 3
            if r == 0:
                return [(0, P, 2 * j, 0)]
            if r == 2:
                return [(0, P, 2 * j + 1, 0)]
            return [(0, 64, 2 * j, P), (64, 64, 2 * j + 1, P)]

        def proj_a_dve(dve):
            seg_dve(dve, "a_v", None)

            def turned(i, T, slot):
                for half in range(2):
                    dve.wait_ge(v_tr, 2 * i + half + 1)
                    for p0, n, h, c0 in v_heads(i):
                        ins = dve.tensor_copy(
                            v_ext[:, 4 * half:4 * half + 4, h, c0:c0 + n],
                            ps[:, 6 + half, :].rearrange("p (s d) -> p s d", s=4)[:, :, p0:p0 + n])
                    ins.then_inc(v_cp, 1)
            T0 = segs["a_q"][0]
            for i in range(6):
                split_lo(dve, T0 + i + 1, (T0 + i + 1) % 2, 8)
                turned(i, T0 + i, (T0 + i) % 2)
            dve.memset(v_ext[:, :, :, DH:DH + 1], 1.0)
            seg_dve(dve, "a_m")
            seg_dve(dve, "a_g")
            seg_dve(dve, "a_k", None, chain=False)

        def proj_a_pe(pe):
            seg_pe(pe, "a_v", ready=normed(0))
            pe.wait_ge(a_ev, 1)
            T0 = segs["a_q"][0]
            for i in range(6):
                pe_tile(pe, T0 + i)
                for half in range(2):
                    if i > 0:
                        pe.wait_ge(v_cp, 2 * i - 1 + half)
                    for s in range(4):
                        mm = pe.transpose(ps[:, 6 + half, s * P:(s + 1) * P],
                                          kT[:, i, (4 * half + s) * P:(4 * half + s + 1) * P], C("ident"))
                    mm.then_inc(v_tr, 1)
            seg_pe(pe, "a_m")
            seg_pe(pe, "a_g")
            seg_pe(pe, "a_k")

        def pe_tile(pe, T):
            slot = T % 2
            pe.wait_ge(w_hi_ready, T + 1)
            pe.wait_ge(w_lo_ready, T + 1)
            pe.wait_ge(tile_free, T - 1)
            for k in range(8):
                for w, a in ((w_hi, h_hi), (w_hi, h_lo), (w_lo, h_hi)):
                    for c in range(3):
                        mm = pe.matmul(ps[:, 3 * slot + c, 0:CH], w[:, slot, k * P:(k + 1) * P],
                                       a[:, k, c * CH:(c + 1) * CH], start=(k == 0 and w is w_hi and a is h_hi),
                                       stop=(k == 7 and w is w_lo))
            mm.then_inc(tile_done, 1)

        at = [wk_at + 8 * N]

        def work(name, shape, dt=F32):
            size = (4 * int(np.prod(shape[1:])) + 31) // 32 * 32
            t = place(name, shape, dt, at=at[0])
            at[0] += size
            return t
        gz = rows2
        p_w = work("p_w", [P, 2, 512])
        p_p = work("p_p", [P, 2, 512])
        sq_b = work("sq_b", [P, 512])
        sq_s = work("sq_s", [65, 512])
        m_rr = work("m_rr", [P, 512])
        acol = work("acol", [P, NT, MH])
        wcol = work("wcol", [P, MH, NT])
        nMT = work("nMT", [P, MH])
        dg = work("dg", [4, 4])
        m_out = work("m_out", [4, 1 + NB])
        sm_in = work("sm_in", [4, NB])
        sm = work("sm", [4, 3 * NB])
        sm_t = work("sm_t", [4, NB])
        smb = work("smb", [P, MH, 3 * NB])
        wT = work("wT", [NB, MH])
        pass
        assert at[0] <= w_hi_at + 16 * DM
        gr_a, gr_d, gr_p = sem("gr_a"), sem("gr_d"), sem("gr_p")
        ml_ld = sem("ml_ld")
        m_nm, m_l, m_s, m_d, m_w, m_p, m_pv = (sem(x) for x in ("m_nm", "m_l", "m_s", "m_d", "m_w", "m_p", "m_pv"))
        m_x, m_sq, m_d2, m_var, m_r, m_o = (sem(x) for x in ("m_x", "m_sq", "m_d2", "m_var", "m_r", "m_o"))
        R0, R1, R2 = gz, rows0, rows1
        one = lambda p0, n: con[p0:p0 + n, _C["ones"][0]:_C["ones"][0] + 1]

        def gates_act(act):
            act.activation(R1[32:36, :], R0[32:36, :], ACT.Abs)
            act.drain()
            act.activation(R1[32:36, :], R1[32:36, :], ACT.Exp, scale=-1.0)
            act.drain()
            act.activation(R1[32:36, :], R1[32:36, :], ACT.Ln, bias=one(32, 4)).then_inc(gr_a, 1)
            act.wait_ge(gr_d, 1)
            act.activation(R1[0:4, 0:SEQ], R1[0:4, 0:SEQ], ACT.Exp, scale=-2.0)
            act.activation(sm[:, :], sm[:, :], ACT.Exp).then_inc(gr_a, 1)
            act.wait_ge(gr_p, 1)
            act.activation(acol[:, :, :], ps[:, 6, 0:NT * MH].rearrange("p (s h) -> p s h", h=MH), ACT.Copy)
            act.activation(nMT[:, :], ps[:, 7, 0:MH], ACT.Copy)
            act.activation(wT[:, :], ps[0:NB, 7, 8:8 + MH], ACT.Copy)
            act.activation(smb[:, :, :], ps[:, 7, 16:16 + MH * 3 * NB].rearrange("p (h n) -> p h n", h=MH), ACT.Copy)
            act.drain()
            for h in range(MH):
                ins = act.activation(wcol[:, h, :], acol[:, :, h], ACT.Exp, bias=nMT[:, h:h + 1])
            ins.then_inc(gr_a, 1)
            act.dma_start(O["o_m"], m_out[:, :]).then_inc(out_s, 16)
            outs[0] += 1

        def gates_dve(dve):
            dve.wait_ge(gr_a, 1)
            dve.scalar_tensor_tensor(out=R2[0:4, :], in0=R0[32:36, :], scalar=0.0, in1=R1[32:36, :],
                                     op0=ALU.min, op1=ALU.subtract)
            dve.memset(R1[0:4, :], 0.0)
            dve.drain()
            dve.wait_ge(ml_ld, 16)
            lf, ig = R2[0:4, SEQ:N], R0[0:4, SEQ:N]
            dve.tensor_tensor(sm_t[:, :], lf, sm_in[:, :], ALU.add)
            dve.drain()
            dve.tensor_tensor(m_out[:, 1:1 + NB], ig, sm_t[:, :], ALU.max)
            dve.drain()
            dve.tensor_tensor(sm[:, 0:NB], ig, m_out[:, 1:1 + NB], ALU.subtract)
            dve.tensor_tensor(sm[:, NB:2 * NB], sm_t[:, :], m_out[:, 1:1 + NB], ALU.subtract)
            dve.tensor_scalar(sm[:, 2 * NB:], m_out[:, 1:1 + NB], -2.0, None, ALU.mult)
            dve.tensor_tensor_scan(R1[0:4, 0:SEQ], R2[0:4, 0:SEQ], R1[0:4, 0:SEQ], 0.0, ALU.add, ALU.add)
            dve.drain()
            dve.tensor_tensor(R0[0:4, 0:SEQ], R0[0:4, 0:SEQ], R1[0:4, 0:SEQ], ALU.subtract)
            dve.drain()
            dve.tensor_tensor_scan(R2[0:4, 0:SEQ], R0[0:4, 0:SEQ], R0[0:4, 0:SEQ], NEG, ALU.max, ALU.max)
            dve.drain()
            dve.tensor_tensor(R1[0:4, 0:SEQ], R1[0:4, 0:SEQ], R2[0:4, 0:SEQ], ALU.add)
            dve.tensor_scalar(R2[0:4, 0:SEQ], R2[0:4, 0:SEQ], -1.0, None, ALU.mult)
            dve.drain()
            dve.tensor_copy(m_out[:, 0:1], R1[0:4, SEQ - 1:SEQ])
            dve.tensor_scalar(dg[:, :], C("ident", 4, 0, 4), R2[0:4, SEQ - 1:SEQ], None, ALU.mult)
            dve.drain()
            dve.sem_inc(gr_d, 1)

        def gates_pe(pe):
            pe.wait_ge(gr_d, 1)
            pe.wait_ge(gr_a, 2)
            for s in range(NT):
                pe.transpose(ps[:, 6, s * MH:(s + 1) * MH], R0[0:4, s * P:(s + 1) * P], C("ident", 4, 0, 4))
            pe.matmul(ps[:, 7, 0:MH], C("ones", 4), dg[:, :], start=True, stop=True)
            pe.transpose(ps[0:NB, 7, 8:8 + MH], sm[:, 0:NB], C("ident", 4, 0, 4))
            for h in range(MH):
                mm = pe.matmul(ps[:, 7, 16 + 24 * h:40 + 24 * h], C("head_rows", 4, h * P, P), sm[:, :],
                               start=True, stop=True, skip_group_check=True)
            mm.then_inc(gr_p, 1)

        units = [(h, c, s) for h in range(MH) for c in range(2) for s in range(4 * c + 4)]
        last_unit = {(h, c): n for n, (h, c, s) in enumerate(units)}
        first_unit = {}
        for n_, (h_, c_, s_) in enumerate(units):
            first_unit.setdefault((h_, c_), n_)

        def span(c, s):
            t0 = max(512 * c, P * s)
            return t0, 512 * (c + 1) - t0

        def parts(h):
            j = h // 2
            return [(3 * j, 0, P), (3 * j + 1, 0, 64)] if h % 2 == 0 else [(3 * j + 2, 0, P), (3 * j + 1, 64, 64)]

        def mlstm_pe(pe):
            def pv(n):
                h, c, s = units[n]
                t0, w = span(c, s)
                o = t0 - 512 * c
                pe.wait_ge(m_p, n + 1)
                if s == 0 and 2 * h + c > 0:
                    pe.wait_ge(m_o, 2 * h + c)
                pe.matmul(ps[:, 2, o:512], v_ext[:, s, h, 0:P], p_p[:, n % 2, 0:w], start=(s == 0),
                          stop=(s == 4 * c + 3), skip_group_check=True)
                pe.matmul(ps[0:65, 3, o:512], v_ext[:, s, h, P:DH + 1], p_p[:, n % 2, 0:w], start=(s == 0),
                          stop=(s == 4 * c + 3), skip_group_check=True).then_inc(m_pv, 1)

            def tail(k):
                h, c = k // 2, k % 2
                if k > 0:
                    pe.wait_ge(m_d2, k)
                pe.matmul(ps[0:65, 7, :], C("head_row64", 4, h * 65, 65), R1[0:4, c * 512:(c + 1) * 512],
                          start=True, stop=True).then_inc(m_x, 1)
                pe.wait_ge(m_sq, k + 1)
                if k > 0:
                    pe.wait_ge(m_r, k)
                pe.matmul(ps[:, 6, :], C("ones"), sq_b[:, :], start=True, stop=False)
                pe.matmul(ps[:, 6, :], C("ones", 64), sq_s[0:64, :], start=False, stop=False)
                pe.wait_ge(m_d2, k + 1)
                pe.matmul(ps[:, 6, :], con[64:65, _C["eps_row"][0]:_C["eps_row"][0] + P], sq_s[64:65, :],
                          start=False, stop=True).then_inc(m_var, 1)

            for n, (h, c, s) in enumerate(units):
                if c == 0 and s == 0:
                    if h:
                        pe.wait_ge(m_w, n)
                        pe.wait_ge(m_p, n)
                    for cc in range(2):
                        mm = pe.matmul(ps[:, 4 + cc, :], C("head_rows", 4, h * P, P), R2[0:4, cc * 512:(cc + 1) * 512],
                                       start=True, stop=True)
                    mm.then_inc(m_nm, 1)
                if n >= 2:
                    pe.wait_ge(m_p, n - 1)
                t0, w = span(c, s)
                for q, (tl, p0, r) in enumerate(parts(h)):
                    mm = pe.matmul(ps[:, n % 2, 0:w], kT[p0:p0 + r, tl, s * P:(s + 1) * P], mix[p0:p0 + r, tl, t0:t0 + w],
                                   start=(q == 0), stop=(q == 1))
                mm.then_inc(m_s, 1)
                if n >= 1:
                    pv(n - 1)
                    if units[n - 1][:2] != (h, c):
                        tail(2 * units[n - 1][0] + units[n - 1][1])
            pv(len(units) - 1)
            tail(2 * MH - 1)

        def mlstm_act(act):
            def tail(k):
                h, c = k // 2, k % 2
                act.wait_ge(m_pv, last_unit[(h, c)] + 1)
                if k > 0:
                    act.wait_ge(m_var, k)
                act.activation(sq_b[:, :], ps[:, 2, :], ACT.Square)
                act.activation(sq_s[0:64, :], ps[0:64, 3, :], ACT.Square)
                act.activation(sq_s[64:65, :], ps[64:65, 3, :], ACT.Square).then_inc(m_sq, 1)
                act.wait_ge(m_var, k + 1)
                if k > 0:
                    act.wait_ge(m_o, k)
                act.activation(m_rr[:, :], ps[:, 6, :], ACT.Ln, scale=1.0 / DH)
                act.drain()
                act.activation(m_rr[:, :], m_rr[:, :], ACT.Exp, scale=-0.5).then_inc(m_r, 1)

            def logs(n):
                h, c, s = units[n]
                if s < 4 * c:
                    return
                t0, w = span(c, s)
                if c == 0 and s == 0:
                    act.wait_ge(m_nm, h + 1)
                if n >= 2:
                    act.wait_ge(m_p, n - 1)
                act.activation(p_w[:, n % 2, 0:w], ps[:, 4 + c, t0 - 512 * c:512], ACT.Identity,
                               bias=acol[:, s, h:h + 1]).then_inc(m_l, 1)

            logs(0)
            for n, (h, c, s) in enumerate(units):
                if n + 1 < len(units) and units[n + 1][0] == h:
                    logs(n + 1)
                t0, w = span(c, s)
                if s >= 4 * c:
                    act.wait_ge(m_d, h * 8 + s + 1)
                    act.activation(p_w[:, n % 2, 0:w], p_w[:, n % 2, 0:w], ACT.Exp).then_inc(m_w, 1)
                else:
                    if n >= 2:
                        act.wait_ge(m_p, n - 1)
                    act.activation(p_w[:, n % 2, 0:w], ps[:, 4 + c, t0 - 512 * c:512], ACT.Exp,
                                   bias=acol[:, s, h:h + 1]).then_inc(m_w, 1)
                if n == last_unit[(h, c)]:
                    tail(2 * h + c)
                if n + 1 < len(units) and units[n + 1][0] != h:
                    logs(n + 1)

        def mlstm_dve(dve):
            def diag(n):
                h, c, s = units[n]
                if s < 4 * c:
                    return
                t0, w = span(c, s)
                dve.wait_ge(m_l, h * 8 + s + 1)
                dve.tensor_tensor(p_w[:, n % 2, 0:w], p_w[:, n % 2, 0:w], C("causal", P, 0, w), ALU.min).then_inc(m_d, 1)

            def tail(k):
                h, c = k // 2, k % 2
                dve.wait_ge(m_x, k + 1)
                dve.wait_ge(m_sq, k + 1)
                dve.tensor_tensor(sq_s[64:65, :], ps[64:65, 7, :], sq_s[64:65, :], ALU.max).then_inc(m_d2, 1)
                dve.wait_ge(m_r, k + 1)
                (tb, _, _), (tl, p0, _) = parts(h)
                cols = slice(c * 512, (c + 1) * 512)
                dve.scalar_tensor_tensor(out=mix[:, tb, cols], in0=ps[:, 2, :], scalar=G("g_hb", h % 2),
                                         in1=m_rr[:, :], op0=ALU.mult, op1=ALU.mult)
                dve.scalar_tensor_tensor(out=mix[p0:p0 + 64, tl, cols], in0=ps[0:64, 3, :],
                                         scalar=G("g_hs", h % 2, 64), in1=m_rr[0:64, :],
                                         op0=ALU.mult, op1=ALU.mult).then_inc(m_o, 1)

            dve.wait_ge(gr_a, 3)
            diag(0)
            for n, (h, c, s) in enumerate(units):
                t0, w = span(c, s)
                if n + 1 < len(units) and units[n + 1][0] == h:
                    diag(n + 1)
                dve.wait_ge(m_w, n + 1)
                dve.wait_ge(m_s, n + 1)
                if n >= 2:
                    dve.wait_ge(m_pv, n - 1)
                dve.tensor_tensor(p_p[:, n % 2, 0:w], p_w[:, n % 2, 0:w], ps[:, n % 2, 0:w], ALU.mult).then_inc(m_p, 1)
                if n + 1 == len(units) or units[n + 1][:2] != (h, c):
                    tail(2 * h + c)
                if n + 1 < len(units) and units[n + 1][0] != h:
                    diag(n + 1)

        kw = place("kw", [P, NT, DH], at=wk_at + 8 * N)
        c_out = place("c_out", [P, MH, 2, DH + 1], at=wk_at + 8 * N + 4 * NT * DH)
        c_t, c_k, c_c, c_e = sem("c_t"), sem("c_k"), sem("c_c"), sem("c_e")

        def state_pe(pe):
            for h in range(MH):
                (tb, _, _), (tl, p0, _) = parts(h)
                if h:
                    pe.wait_ge(c_k, h)
                for s in range(NT):
                    pe.transpose(ps[:, s // 4, (s % 4) * P:(s % 4 + 1) * P], kT[:, tb, s * P:(s + 1) * P], C("ident"))
                for s in range(NT):
                    mm = pe.transpose(ps[:, 2, s * 64:(s + 1) * 64], kT[p0:p0 + 64, tl, s * P:(s + 1) * P],
                                      con[p0:p0 + 64, _C["ident"][0] + p0:_C["ident"][0] + p0 + 64])
                mm.then_inc(c_t, 1)
                pe.wait_ge(c_k, h + 1)
                if h:
                    pe.wait_ge(c_e, h)
                for s in range(NT):
                    pe.matmul(ps[:, 3, 0:DH + 1], kw[:, s, 0:P], v_ext[:, s, h, :], start=(s == 0), stop=(s == NT - 1))
                for s in range(NT):
                    mm = pe.matmul(ps[0:64, 4, 0:DH + 1], kw[:, s, P:DH], v_ext[:, s, h, :], start=(s == 0),
                                   stop=(s == NT - 1))
                mm.then_inc(c_c, 1)

        def state_dve(dve):
            for h in range(MH):
                dve.wait_ge(c_t, h + 1)
                if h:
                    dve.wait_ge(c_c, h)
                for q in range(2):
                    dve.tensor_tensor(kw[:, 4 * q:4 * q + 4, 0:P], ps[:, q, :].rearrange("p (s d) -> p s d", s=4),
                                      wcol[:, h, 4 * q:4 * q + 4].unsqueeze(2).to_broadcast([P, 4, P]), ALU.mult)
                dve.tensor_tensor(kw[:, :, P:DH], ps[:, 2, :].rearrange("p (s d) -> p s d", s=8),
                                  wcol[:, h, :].unsqueeze(2).to_broadcast([P, 8, 64]), ALU.mult).then_inc(c_k, 1)

        def state_act(act):
            for h in range(MH):
                act.wait_ge(c_c, h + 1)
                act.activation(c_out[:, h, 0, :], ps[:, 3, 0:DH + 1], ACT.Copy)
                act.activation(c_out[0:64, h, 1, :], ps[0:64, 4, 0:DH + 1], ACT.Copy).then_inc(c_e, 1)
            act.wait_ge(c_e, MH)
            act.dma_start(O["o_cb"], c_out[:, :, 0, :]).then_inc(out_s, 16)
            act.dma_start(O["o_cs"], c_out[0:64, :, 1, :]).then_inc(out_s, 16)
            outs[0] += 2
            act.wait_ge(out_s, 16 * outs[0])

        at[0] = wk_at
        cs_a = work("cs_a", [P, 2, NB * DH])
        cs_b = place("cs_b", [P, 2, NB * DH], at=a2 + 24 * N)
        cs = [cs_a[:, 0, :], cs_a[:, 1, :], cs_b[:, 0, :], cs_b[:, 1, :]]
        vdiag = work("vdiag", [NB, NB, DH])
        k_s = work("k_s", [NB, DH])
        vw_s = work("vw_s", [NB, DH])
        nb_ = work("nb_", [P, MH, NB])
        ns_ = work("ns_", [P, 2, NB])
        kwb = work("kwb", [P, MH, NB])
        kws = work("kws", [P, 2, NB])
        num = work("num", [P, 2, MH * NB])
        nsq = work("nsq", [P, 2, MH * NB])
        den2 = work("den2", [P, MH * NB])
        s_rr = work("s_rr", [P, MH * NB])
        pass
        assert at[0] <= wk_at + 8 * N + 14 * 1024
        cs_in, cs_w = [sem(f"cs_in{b}") for b in range(4)], sem("cs_w")
        cs_o, n_in = [sem(f"cs_o{b}") for b in range(4)], sem("n_in")
        e_t, e_k, e_v, e_kv, e_q, e_f, e_g = (sem(x) for x in ("e_t", "e_k", "e_v", "e_kv", "e_q", "e_f", "e_g"))

        def cpart(n):
            h, q = n // 2, n % 2
            return parts(h)[q]

        def samples_sp(sp):
            sp.wait_ge(fence_s, 3 * 4)
            sp.dma_start(nb_[:, :, :], A["n_b"]).then_inc(n_in, 16)
            sp.dma_start(ns_[:, :, :], A["n_s"]).then_inc(n_in, 16)
            for n in range(8):
                _, p0, r = cpart(n)
                if n >= 4:
                    sp.wait_ge(cs_o[n % 4], 16)
                    sp.wait_ge(e_q, n - 3)
                sp.dma_start(cs[n % 4][p0:p0 + r, :], A["c_b" if n % 2 == 0 else "c_s"][n // 2]).then_inc(cs_in[n % 4], 16)

        def samples_pe(pe):
            for n in range(8):
                h, q = n // 2, n % 2
                tl, p0, r = parts(h)[q]
                if q == 0:
                    if h:
                        pe.wait_ge(e_k, h)
                        pe.wait_ge(e_v, h)
                    for qq, (tt, pp, rr) in enumerate(parts(h)):
                        idt = con[pp:pp + rr, _C["ident"][0] + pp:_C["ident"][0] + pp + rr]
                        c0 = P * qq
                        pe.transpose(ps[0:NB, 4, c0:c0 + rr], kT[pp:pp + rr, tt, SEQ:N], idt)
                        mm = pe.transpose(ps[0:NB, 7, c0:c0 + rr], vsT[pp:pp + rr, tt, :], idt)
                    mm.then_inc(e_t, 1)
                    pe.wait_ge(e_k, h + 1)
                    pe.wait_ge(e_v, h + 1)
                if n:
                    pe.wait_ge(cs_w, n)
                for b in range(4):
                    mm = pe.matmul(ps[p0:p0 + r, b, 0:2 * DH], k_s[:, P * q:P * q + r], vdiag[:, 2 * b:2 * b + 2, :],
                                   start=True, stop=True)
                mm.then_inc(e_kv, 1)
                pe.wait_ge(cs_w, n + 1)
                for b in range(NB):
                    for e, c0, w in ((0, 0, P), (1, P, 64)):
                        col = q * MH * NB + h * NB + b
                        mm = pe.matmul(ps[0:w, 5 + e, col:col + 1],
                                       cs[n % 4][p0:p0 + r, b * DH + c0:b * DH + c0 + w], mix[p0:p0 + r, tl, SEQ + b:SEQ + b + 1],
                                       start=True, stop=True)
                mm.then_inc(e_q, 1)
            pe.wait_ge(e_f, 1)
            for h in range(MH):
                pe.matmul(ps[:, 0, h * NB:(h + 1) * NB], C("ones"), kwb[:, h, :], start=True, stop=False)
                pe.matmul(ps[:, 0, h * NB:(h + 1) * NB], C("half_rows", P, P * (h % 2), P), kws[:, h // 2, :],
                          start=False, stop=True)
            pe.matmul(ps[:, 1, 0:MH * NB], C("ones"), nsq[:, 0, :], start=True, stop=False)
            pe.matmul(ps[:, 1, 0:MH * NB], C("ones", 64), nsq[0:64, 1, :], start=False, stop=True).then_inc(e_g, 1)

        def samples_act(act):
            for n in range(8):
                h, q = n // 2, n % 2
                _, p0, r = parts(h)[q]
                if q == 0:
                    act.wait_ge(e_t, h + 1)
                    if h:
                        act.wait_ge(e_kv, 2 * h)
                    act.activation(k_s[:, :], ps[0:NB, 4, 0:DH], ACT.Copy).then_inc(e_k, 1)
                act.wait_ge(cs_w, n + 1)
                act.dma_start(O["o_scb" if q == 0 else "o_scs"][h], cs[n % 4][p0:p0 + r, :]).then_inc(cs_o[n % 4], 16)
            act.wait_ge(e_g, 1)
            act.activation(den2[:, :], ps[:, 0, 0:MH * NB], ACT.Square).then_inc(e_g, 1)
            act.wait_ge(e_f, 2)
            act.activation(s_rr[:, :], s_rr[:, :], ACT.Ln)
            act.drain()
            act.activation(s_rr[:, :], s_rr[:, :], ACT.Exp, scale=-0.5).then_inc(e_g, 1)
            act.dma_start(O["o_nb"], nb_[:, :, :]).then_inc(out_s, 16)
            act.dma_start(O["o_ns"], ns_[:, :, :]).then_inc(out_s, 16)
            outs[0] += 2
            act.wait_ge(out_s, 16 * outs[0])
            for b in range(4):
                act.wait_ge(cs_o[b], 16 * 2)

        def samples_dve(dve):
            dve.wait_ge(n_in, 32)
            kB = kT[:, :, SEQ:N].rearrange("p (j r) b -> p j r b", r=3)
            qB = mix[:, 0:6, SEQ:N].rearrange("p (j r) b -> p j r b", r=3)
            w_, dec, em = smb[:, :, 0:NB], smb[:, :, NB:2 * NB], smb[:, :, 2 * NB:]
            dve.tensor_tensor(nb_[:, :, :], nb_[:, :, :], dec, ALU.mult)
            for r in range(2):
                rows = slice(64 * r, 64 * r + 64)
                dve.tensor_tensor(kwb[:, r::2, :], kB[:, :, 2 * r, :], w_[:, r::2, :], ALU.mult)
                dve.tensor_tensor(kws[rows], kB[rows, :, 1, :], w_[rows, r::2, :], ALU.mult)
                dve.tensor_tensor(ns_[rows], ns_[rows], dec[rows, r::2, :], ALU.mult)
            dve.drain()
            dve.tensor_tensor(nb_[:, :, :], nb_[:, :, :], kwb[:, :, :], ALU.add)
            dve.tensor_tensor(ns_[:, :, :], ns_[:, :, :], kws[:, :, :], ALU.add)
            dve.drain()
            for r in range(2):
                dve.tensor_tensor(kwb[:, r::2, :], qB[:, :, 2 * r, :], nb_[:, r::2, :], ALU.mult)
            dve.tensor_tensor(kws[:, :, :], qB[:, :, 1, :], ns_[:, :, :], ALU.mult)
            for n in range(8):
                h, q = n // 2, n % 2
                tl, p0, r = parts(h)[q]
                if q == 0:
                    dve.wait_ge(e_t, h + 1)
                    dve.tensor_scalar(vw_s[:, :], ps[0:NB, 7, 0:DH], wT[:, h:h + 1], None, ALU.mult)
                    dve.drain()
                    if h:
                        dve.wait_ge(e_kv, 2 * h)
                    dve.tensor_tensor(vdiag[:, :, :], vw_s[:, :].unsqueeze(1).to_broadcast([NB, NB, DH]),
                                      C("eye8", NB).unsqueeze(2).to_broadcast([NB, NB, DH]), ALU.mult).then_inc(e_v, 1)
                dve.wait_ge(cs_in[n % 4], 16 * (n // 4 + 1))
                c3 = cs[n % 4][p0:p0 + r, :].rearrange("p (b e) -> p b e", b=NB)
                dve.tensor_tensor(c3, c3, dec[p0:p0 + r, h, :].unsqueeze(2).to_broadcast([r, NB, DH]), ALU.mult)
                dve.drain()
                dve.wait_ge(e_kv, n + 1)
                c4 = cs[n % 4][p0:p0 + r, :].rearrange("p (b e) -> p b e", b=4)
                dve.tensor_tensor(c4, c4, ps[p0:p0 + r, 0:4, 0:2 * DH], ALU.add).then_inc(cs_w, 1)
            dve.wait_ge(e_q, 8)
            X = MH * NB
            for e, w in ((0, P), (1, 64)):
                dve.tensor_copy(num[0:w, e, :], ps[0:w, 5 + e, 0:X])
            dve.drain()
            for e, w in ((0, P), (1, 64)):
                dve.tensor_tensor(num[0:w, e, :], num[0:w, e, :], ps[0:w, 5 + e, X:2 * X], ALU.add)
            dve.drain()
            for e, w in ((0, P), (1, 64)):
                dve.tensor_tensor(nsq[0:w, e, :], num[0:w, e, :], num[0:w, e, :], ALU.mult)
            dve.drain()
            dve.sem_inc(e_f, 1)
            dve.wait_ge(e_g, 2)
            d3 = den2[:, :].rearrange("p (h b) -> p h b", h=MH)
            dve.tensor_tensor(d3, d3, em, ALU.max)
            dve.tensor_scalar(s_rr[:, :], ps[:, 1, 0:X], 1.0 / DH, None, ALU.mult)
            dve.drain()
            dve.scalar_tensor_tensor(out=s_rr[:, :], in0=den2[:, :], scalar=EPS, in1=s_rr[:, :], op0=ALU.mult,
                                     op1=ALU.add).then_inc(e_f, 1)
            dve.wait_ge(e_g, 3)
            for h in range(MH):
                (tb, _, _), (tl, p0, _) = parts(h)
                hc = slice(h * NB, (h + 1) * NB)
                dve.scalar_tensor_tensor(out=mix[:, tb, SEQ:N], in0=num[:, 0, hc], scalar=G("g_hb", h % 2),
                                         in1=s_rr[:, hc], op0=ALU.mult, op1=ALU.mult)
                dve.scalar_tensor_tensor(out=mix[p0:p0 + 64, tl, SEQ:N], in0=num[0:64, 1, hc],
                                         scalar=G("g_hs", h % 2, 64), in1=s_rr[0:64, hc], op0=ALU.mult, op1=ALU.mult)

        o_sg = place("o_sg", [P, 2, N], at=a2)
        og_s = sem("og_s")

        def ogate_act(act):
            def evac(i, T, slot, j):
                act.wait_ge(tile_done, T + 1)
                b = 1 - slot
                act.wait_ge(tile_free, T - 1)
                act.activation(three(o_sg[:, b, :]), acc(slot), ACT.Sigmoid).then_inc(og_s, 1)
            seg_act(act, "a_o", evac, first=True, chain=False)

        def ogate_dve(dve):
            def evac(i, T, slot, j):
                dve.wait_ge(og_s, i + 1)
                b = 1 - slot
                dve.tensor_tensor(mix[:, i, :], mix[:, i, :], o_sg[:, b, :], ALU.mult).then_inc(tile_free, 1)
            seg_dve(dve, "a_o", evac, first=True, chain=False)

        b2 = a2 + 32768
        mk_s = place("mk_s", [P, NB, 2, MEM], at=a2)
        mv_s = place("mv_s", [P, NB, 2, MEM], at=a2 + 16384)
        hq_sq = place("hq_sq", [P, 2, N], at=b2)
        hq_rt = place("hq_rt", [P, 2, N], at=b2 + 8 * N)
        ma_p = place("ma_p", [P, 2, MH, MEM], at=b2)
        ma_pt = place("ma_pt", [P, 8, P], at=b2 + 8192)
        ma_f = place("ma_f", [P, 4, 2, MH], at=b2 + 12288)
        qz = place("qz", [P, 2, NB, 32], at=b2 + 12416)
        assert b2 + 12416 + 2048 <= arena_end and b2 + 16 * N <= arena_end
        (ma_ld, ma_s, ma_m, ma_e, ma_n, ma_t, ma_c, ma_pv, ma_o, ma_z) = (
            sem(x) for x in ("ma_ld", "ma_s", "ma_m", "ma_e", "ma_n", "ma_t", "ma_c", "ma_pv", "ma_o", "ma_z"))
        U = NT + 1

        def mem_load(sp, l):
            sp.dma_start(mk_s[:, :, :, :], A["c_mk"][l]).then_inc(ma_ld, 16)
            sp.dma_start(mv_s[:, :, :, :], A["c_mv"][l]).then_inc(ma_ld, 16)

        def attend_pe(pe, l):
            base = l * U

            def scores(i):
                if i >= 2:
                    pe.wait_ge(ma_e, base + i - 1)
                if i < NT:
                    for h in range(MH):
                        p0 = 64 * (h % 2)
                        mm = pe.matmul(ps[:, 2 * (i % 2) + h % 2, (h // 2) * MEM:(h // 2 + 1) * MEM],
                                       mix[p0:p0 + 64, 6 + h // 2, i * P:(i + 1) * P], mem_kT[p0:p0 + 64, l, h // 2, :],
                                       start=True, stop=True)
                else:
                    pe.wait_ge(ma_z, l + 1)
                    pe.wait_ge(ma_ld, 32 * (l + 1))
                    for j in range(2):
                        for b in range(NB):
                            mm = pe.matmul(ps[0:32, 2 * (i % 2), 0:MEM], qz[:, j, b, :], mk_s[:, b, j, :],
                                           start=(j == 0 and b == 0), stop=(j == 1 and b == NB - 1))
                mm.then_inc(ma_s, 1)

            def turn(i):
                pe.wait_ge(ma_n, base + i + 1)
                if i:
                    pe.wait_ge(ma_c, 2 * (base + i))
                if i < NT:
                    for h in range(MH):
                        for m in range(2):
                            mm = pe.transpose(ps[:, 4 + h // 2, ((h % 2) * 2 + m) * P:((h % 2) * 2 + m + 1) * P],
                                              ma_p[:, i % 2, h, m * P:(m + 1) * P], C("ident"))
                else:
                    for m in range(2):
                        mm = pe.transpose(ps[:, 4 + m, 0:32], ma_p[0:32, i % 2, 0, m * P:(m + 1) * P], C("ident", 32, 0, 32))
                mm.then_inc(ma_t, 1)

            def values(i):
                pe.wait_ge(ma_c, 2 * (base + i + 1))
                if i >= 2:
                    pe.wait_ge(ma_o, base + i - 1)
                if i < NT:
                    for h in range(MH):
                        p0 = 64 * (h % 2)
                        for m in range(2):
                            mm = pe.matmul(ps[p0:p0 + 64, 6 + i % 2, (h // 2) * P:(h // 2 + 1) * P],
                                           mem_v[:, l, m, h * HD:(h + 1) * HD], ma_pt[:, 2 * h + m, :],
                                           start=(m == 0), stop=(m == 1))
                else:
                    for j in range(2):
                        for b in range(NB):
                            for m in range(2):
                                mm = pe.matmul(ps[:, 6 + i % 2, 32 * j + 4 * b:32 * j + 4 * b + 4],
                                               mv_s[:, b, m, j * P:(j + 1) * P], ma_pt[:, m, 4 * b:4 * b + 4],
                                               start=(m == 0), stop=(m == 1))
                mm.then_inc(ma_pv, 1)

            scores(0)
            scores(1)
            for i in range(U):
                if i + 2 < U:
                    scores(i + 2)
                turn(i)
                if i:
                    values(i - 1)
            values(U - 1)

        def attend_act(act, l):
            base = l * U

            def exps(i):
                act.wait_ge(ma_m, base + i + 1)
                if i >= 2:
                    act.wait_ge(ma_t, base + i - 1)
                rows, hs = (P, MH) if i < NT else (32, 1)
                for h in range(hs):
                    c = (h % 2) * 2 + h // 2
                    ins = act.activation(ma_p[0:rows, i % 2, h, :], ps[0:rows, 2 * (i % 2) + h % 2, (h // 2) * MEM:(h // 2 + 1) * MEM],
                                         ACT.Exp, bias=ma_f[0:rows, 1, i % 2, c:c + 1], scale=0.125,
                                         accum_out=ma_f[0:rows, 2, i % 2, c:c + 1])
                ins.then_inc(ma_e, 1)

            def turned(i):
                act.wait_ge(ma_t, base + i + 1)
                if i:
                    act.wait_ge(ma_pv, base + i)
                n = P if i < NT else 32
                t = 4 if i < NT else 1
                act.activation(ma_pt[:, 0:t, 0:n], ps[:, 4, 0:t * n].rearrange("p (m t) -> p m t", m=t),
                               ACT.Copy).then_inc(ma_c, 1)

            def outputs(i):
                act.wait_ge(ma_pv, base + i + 1)
                if i < NT:
                    act.activation(mix[:, 6:8, i * P:(i + 1) * P], ps[:, 6 + i % 2, 0:256].rearrange("p (j t) -> p j t", j=2),
                                   ACT.Copy).then_inc(ma_o, 1)
                else:
                    for h in range(MH):
                        p0, j = 64 * (h % 2), h // 2
                        ins = act.activation(mix[p0:p0 + 64, 6 + j, SEQ:N],
                                             ps[p0:p0 + 64, 6 + i % 2, 32 * j + h:32 * j + 32:4], ACT.Copy)
                    ins.then_inc(ma_o, 1)

            exps(0)
            for i in range(U):
                if i:
                    turned(i - 1)
                if i >= 2:
                    outputs(i - 2)
                if i + 1 < U:
                    exps(i + 1)
            turned(U - 1)
            outputs(U - 2)
            outputs(U - 1)

        def attend_dve(dve, l):
            base = l * U
            dve.memset(qz[:, :, :, :], 0.0)
            dve.drain()
            for h in range(MH):
                p0, j = 64 * (h % 2), h // 2
                q2 = qz[:, j, :, :].rearrange("p b c -> p (b c)")
                dve.tensor_copy(q2[p0:p0 + 64, h:h + 36 * (NB - 1) + 1:36], mix[p0:p0 + 64, 6 + j, SEQ:N])
            dve.drain()
            dve.sem_inc(ma_z, 1)

            def maxes(i):
                dve.wait_ge(ma_s, base + i + 1)
                rows, hs = (P, MH) if i < NT else (32, 1)
                src = (ps[:, 2 * (i % 2):2 * (i % 2) + 2, :].rearrange("p a (h m) -> p (a h) m", h=2) if i < NT
                       else ps[0:32, 2 * (i % 2), 0:MEM].unsqueeze(1))
                dve.tensor_reduce(ma_f[0:rows, 0, i % 2, 0:hs], src, AX, ALU.max)
                dve.drain()
                dve.tensor_scalar(ma_f[0:rows, 1, i % 2, 0:hs], ma_f[0:rows, 0, i % 2, 0:hs], -0.125, None,
                                  ALU.mult).then_inc(ma_m, 1)

            def norm(i):
                rows, hs = (P, MH) if i < NT else (32, 1)
                dve.wait_ge(ma_e, base + i + 1)
                dve.reciprocal(ma_f[0:rows, 3, i % 2, 0:hs], ma_f[0:rows, 2, i % 2, 0:hs])
                dve.drain()
                for h in range(hs):
                    c = (h % 2) * 2 + h // 2
                    ins = dve.tensor_scalar(ma_p[0:rows, i % 2, h, :], ma_p[0:rows, i % 2, h, :],
                                            ma_f[0:rows, 3, i % 2, c:c + 1], None, ALU.mult)
                ins.then_inc(ma_n, 1)

            def turned(i):
                dve.wait_ge(ma_t, base + i + 1)
                if i:
                    dve.wait_ge(ma_pv, base + i)
                if i < NT:
                    dve.tensor_copy(ma_pt[:, 4:8, :], ps[:, 5, :].rearrange("p (m t) -> p m t", m=4)).then_inc(ma_c, 1)
                else:
                    dve.tensor_copy(ma_pt[:, 1, 0:32], ps[:, 5, 0:32]).then_inc(ma_c, 1)

            maxes(0)
            maxes(1)
            for i in range(U):
                norm(i)
                if i:
                    turned(i - 1)
                if i + 2 < U:
                    maxes(i + 2)
            turned(U - 1)

        def add_x(dve, name, first=False, chain=True, norm=None):
            if norm is not None:
                dve.memset(n_buf[norm][2][:, :], 0.0)

            def evac(i, T, slot, j):
                dve.wait_ge(tile_done, T + 1)
                dve.tensor_tensor(three(xT[:, i, :]), three(xT[:, i, :]), acc(slot), ALU.add).then_inc(tile_free, 1)
                if norm is not None:
                    square_dve(dve, norm, i, (slot - segs[name][0]) % 2)
            seg_dve(dve, name, evac, first, chain)

        def sum_x(act, name, norm, first=False, chain=True):
            def evac(i, T, slot, j):
                act.wait_ge(tile_free, T + 1)
                square_act(act, norm, i, (slot - segs[name][0]) % 2)
            seg_act(act, name, evac, first, chain)

        f_h = sem("f_h")
        f_n = {"act": 0, "dve": 0, "pe": 0}

        def ffn_act(act, l):
            for q in range(3):
                name = f"gu{l}{q}"
                T0, n = segs[name][:2]
                base = f_n["act"]

                def evac(i, T, slot, j, par=T0 % 2):
                    if slot == par:
                        act.wait_ge(tile_done, T + 1)
                        act.wait_ge(tile_free, T)
                        act.activation(three(f_silu[:, :]), acc(slot), ACT.Silu).then_inc(tile_free, 1)
                    else:
                        act.wait_ge(tile_free, T + 1)
                        act.activation(hid_hi[:, j, :], f_t[:, :], ACT.Copy).then_inc(f_h, 1)
                seg_act(act, name, evac)
                f_n["act"] += n // 2
                if q == 2 and l == 0:
                    sum_x(act, f"dn{l}{q}", 2)
                else:
                    seg_act(act, f"dn{l}{q}", None, chain=(q < 2))

        def ffn_dve(dve, l):
            for q in range(3):
                name = f"gu{l}{q}"
                T0, n = segs[name][:2]
                base = f_n["dve"]

                def evac(i, T, slot, j, base=base, par=T0 % 2):
                    if slot == par:
                        return
                    dve.wait_ge(tile_free, T)
                    dve.wait_ge(tile_done, T + 1)
                    dve.tensor_tensor(three(f_t[:, :]), acc(slot), three(f_silu[:, :]), ALU.mult).then_inc(tile_free, 1)
                    dve.drain()
                    dve.wait_ge(f_h, j + (base + 1))
                    dve.tensor_tensor(hid_lo[:, j, :], f_t[:, :], hid_hi[:, j, :].bitcast(F32),
                                      ALU.subtract).then_inc(hid_ready, 1)
                seg_dve(dve, name, evac)
                f_n["dve"] += n // 2
                add_x(dve, f"dn{l}{q}", chain=(q < 2 or l == 0), norm=2 if q == 2 and l == 0 else None)

        def ffn_pe(pe, l):
            for q in range(3):
                seg_pe(pe, f"gu{l}{q}", ready=normed(1 if l == 0 else 4) if q == 0 else None)
                f_n["pe"] += segs[f"gu{l}{q}"][1] // 2
                n = segs[f"gu{l}{q}"][1] // 2
                seg_pe(pe, f"dn{l}{q}", hid_hi, hid_lo, ready=lambda k, f=f_n["pe"] - n: (hid_ready, f + k + 1))

        h_at = x_end
        h_end = h_at + 8 * KC * N

        def pack(at, name, shape, dt=F32):
            size = (4 * int(np.prod(shape[1:])) + 31) // 32 * 32
            t = place(name, shape, dt, at=at[0])
            at[0] += size
            return t

        k_at = [a2]
        kk = pack(k_at, "kk", [80, 2, 2, SEQ])
        vv = pack(k_at, "vv", [P, 2, NT, P])
        bias = pack(k_at, "bias", [P, NH, 256])
        cbias = pack(k_at, "cbias", [P, NH, 16])
        ckp = pack(k_at, "ckp", [64, 2, 64])
        cvp = pack(k_at, "cvp", [64, P])
        ck_s = pack(k_at, "ck_s", [P, NB, 64])
        cv_s = pack(k_at, "cv_s", [64, NB, P])
        kvn = pack(k_at, "kvn", [P, 6, NB])
        pass
        assert k_at[0] <= arena_end
        p_at = [h_at]
        w1 = pack(p_at, "w1", [P, 2, 16, P])
        xp = pack(p_at, "xp", [P, 2, 2, 2, 512])
        pages = pack(p_at, "pages", [P, 2, 4, 512])
        w2 = pack(p_at, "w2", [P, 2, HD])
        posT = pack(p_at, "posT", [P, 2, 16])
        b2r = pack(p_at, "b2r", [1, 256])
        hb = pack(p_at, "hb", [P, 2])
        hid = pack(p_at, "hid", [P, 2, 2, 126])
        g_u = pack(p_at, "g_u", [P, 4, 126])
        cko = pack(p_at, "cko", [64, 9, 2, P])
        ckq = pack(k_at, "ckq", [64, 18, HD])
        ckr = pack(p_at, "ckr", [64, 2, 18])
        gkr = pack(p_at, "gkr", [64, HD])
        pt_s = pack(p_at, "pt_s", [1, 64], I32)
        pass
        assert p_at[0] <= h_end
        o_at = [h_at + 12288]
        oh = pack(o_at, "oh", [33, 16 * P + 384])
        tab = pack(o_at, "tab", [33, NH])
        line = pack(o_at, "line", [NH, 384])
        anti = pack(o_at, "anti", [P, P])
        braw = place("braw", [P, NH, 256], at=h_at)
        scratch = nc.dram_tensor("line_dram", (NH, 384), F32)
        kv_e = sem("kv_e")
        b_ld, b_pe, b_ac, b_dm, b_br = sem("b_ld"), sem("b_pe"), sem("b_ac"), sem("b_dm"), sem("b_br")
        kv_t, kv_c = sem("kv_t"), sem("kv_c")

        def kvproj_act(act):
            def evac(i, T, slot, j):
                act.wait_ge(tile_done, T + 1)
                act.activation(three(mix[:, i, :]), acc(slot), ACT.Copy).then_inc(tile_free, 1)
            seg_act(act, "kv", evac, chain=False)

        def bias_sp(sp):
            sp.dma_start(oh[:, :], A["oh"]).then_inc(b_ld, 16)
            sp.dma_start(tab[0:32, :], A["table"]).then_inc(b_ld, 16)
            sp.dma_start(anti[:, :], A["anti"]).then_inc(b_ld, 16)
            for br in range(2):
                for g in range(2):
                    sp.dma_start(kk[64:80, br, g, :], A["blocks"]).then_inc(b_ld, 16)
            sp.wait_ge(b_ac, 1)
            sp.dma_start(scratch.ap(), line[:, :]).then_inc(b_dm, 16)
            sp.wait_ge(b_dm, 16)
            sp.dma_start(braw[:, :, :], bass.AP(tensor=scratch, offset=0, ap=[[1, P], [384, NH], [1, 256]])).then_inc(b_dm, 16)

        def bias_pe(pe):
            pe.wait_ge(b_ld, 16 * 7)
            pe.wait_ge(b_br, 1)
            pe.matmul(ps[0:NH, 0, 0:384], tab[:, :], oh[:, 16 * P:16 * P + 384], start=True, stop=True).then_inc(b_pe, 1)
            for u in range(16):
                mm = pe.matmul(ps[:, 1, u * NH:(u + 1) * NH], oh[:, u * P:(u + 1) * P], tab[:, :], start=True, stop=True)
            mm.then_inc(b_pe, 1)
            pe.wait_ge(b_dm, 32)
            for q in range(6):
                mm = pe.matmul(ps[:, 2 + q, :], anti[:, :], braw[:, 2 * q:2 * q + 2, :], start=True, stop=True)
            mm.then_inc(b_pe, 1)

        def bias_act(act):
            act.wait_ge(b_pe, 1)
            act.activation(line[:, :], ps[0:NH, 0, 0:384], ACT.Copy).then_inc(b_ac, 1)
            act.wait_ge(b_pe, 2)
            act.activation(cbias[:, :, :], ps[:, 1, 0:16 * NH].rearrange("p (u h) -> p h u", h=NH), ACT.Copy)
            act.wait_ge(b_pe, 3)
            for q in range(3):
                act.activation(bias[:, 2 * q:2 * q + 2, :], ps[:, 2 + q, :].rearrange("p (h c) -> p h c", h=2), ACT.Copy)

        def bias_dve(dve):
            dve.memset(tab[32:33, :], NEG).then_inc(b_br, 1)
            dve.wait_ge(b_pe, 3)
            for q in range(3, 6):
                dve.tensor_copy(bias[:, 2 * q:2 * q + 2, :], ps[:, 2 + q, :].rearrange("p (h c) -> p h c", h=2))

        kn_sq = place("kn_sq", [P, 2, N], at=h_at + 12288)
        kn_rt = place("kn_rt", [P, 2, N], at=h_at + 12288 + 8 * N)

        def keys_act(act):
            tl = lambda t: mix[:, 2 + 2 * t, :]
            hnorm_act(act, tl, 2, CH, 3, kn_sq, kn_rt)
            act.wait_ge(hn_o, hn_base["act"])
            act.activation(kvn[:, :, :], mix[:, 0:6, SEQ:N], ACT.Copy)
            for br in range(2):
                for g in range(2):
                    ins = act.activation(kk[0:64, br, g, :], mix[64 * g:64 * g + 64, 2 + 2 * br, 0:SEQ], ACT.Copy)
            ins.then_inc(kv_e, 1)
            act.dma_start(O["o_kv"], mix[:, 0:6, :]).then_inc(out_s, 16)
            outs[0] += 1
            for br in range(2):
                for half in range(2):
                    n = 2 * br + half
                    act.wait_ge(kv_t, n + 1)
                    act.activation(vv[:, br, 4 * half:4 * half + 4, :],
                                   ps[:, 6 + half, :].rearrange("p (s d) -> p s d", s=4), ACT.Copy).then_inc(kv_c, 1)

        def keys_dve(dve):
            tl = lambda t: mix[:, 2 + 2 * t, :]
            hnorm_dve(dve, tl, tl, 2, N, lambda t: G("g_k_slc" if t == 0 else "g_k_win"), kn_rt)

        def keys_pe(pe):
            hnorm_pe(pe, 2, CH, 3, kn_sq)
            for br in range(2):
                for half in range(2):
                    if br:
                        pe.wait_ge(kv_c, 2 * br + half - 1)
                    for s in range(4):
                        mm = pe.transpose(ps[:, 6 + half, s * P:(s + 1) * P],
                                          mix[:, 3 + 2 * br, (4 * half + s) * P:(4 * half + s + 1) * P], C("ident"))
                    mm.then_inc(kv_t, 1)

        NS = 9
        z_ld, z_pg = sem("z_ld"), [sem("z_pg0"), sem("z_pg1")]
        z_x, z_t, z_h, z_g, z_o, z_oc, z_pe0, z_hb = (sem(x) for x in ("z_x", "z_t", "z_h", "z_g", "z_o", "z_oc", "z_pe0", "z_hb"))
        z_u, z_th, z_n, z_n2, z_nt, z_nc = (sem(x) for x in ("z_u", "z_th", "z_n", "z_n2", "z_nt", "z_nc"))

        def cmp_sp(sp):
            sp.dma_start(w1[:, :, :, :], A["w1"]).then_inc(z_ld, 16)
            sp.dma_start(w2[:, :, :], A["w2"]).then_inc(z_ld, 16)
            sp.dma_start(posT[:, :, :], A["posT"]).then_inc(z_ld, 16)
            sp.dma_start(b2r[:, :], A["b2r"]).then_inc(z_ld, 16)
            sp.dma_start(gkr[:, :], A["gkr"]).then_inc(z_ld, 16)
            sp.dma_start(pt_s[:, :], A["pt"]).then_inc(b_dm, 16)
            sp.wait_ge(b_dm, 48)
            for b in range(NB):
                if b >= 2:
                    sp.wait_ge(z_t, 4 * (b - 1))
                for pg in range(8):
                    v = sp.value_load(pt_s[0:1, b * 8 + pg:b * 8 + pg + 1], min_val=0, max_val=A["cmp"].shape[0] - 1)
                    sp.dma_start(pages[64 * (pg % 2):64 * (pg % 2) + 64, b % 2, pg // 2, :], A["cmp"][v]).then_inc(z_pg[b % 2], 16)

        def cmp_pe(pe):
            pe.wait_ge(z_ld, 80)
            for c in range(2):
                for u in range(16):
                    mm = pe.matmul(ps[:, 7, c:c + 1], w1[:, c, u, :], posT[:, c, u:u + 1], start=(u == 0), stop=(u == 15))
            mm.then_inc(z_pe0, 1)

            def turn(s):
                pe.wait_ge(z_pg[(s - 1) % 2], 16 * 8 * ((s - 1) // 2 + 1))
                for c in range(2):
                    for g in range(2):
                        k = 4 * (s - 1) + 2 * c + g
                        if k >= 2:
                            pe.wait_ge(z_x, 4 + k - 1)
                        for q in range(4):
                            o = (2 * c + g) * P
                            mm = pe.transpose(ps[:, k % 2, q * P:(q + 1) * P], pages[:, (s - 1) % 2, q, o:o + P], C("ident"))
                        mm.then_inc(z_t, 1)

            def hidden(s):
                pe.wait_ge(z_x, 4 * (s + 1))
                for c in range(2):
                    n = 2 * s + c
                    if n >= 2:
                        pe.wait_ge(z_u, n - 1)
                    for u in range(16):
                        mm = pe.matmul(ps[:, 2 + c, 0:126].rearrange("p (g n) -> p g n", g=2), w1[:, c, u, :],
                                       xp[:, s % 2, c, :, u:u + 8 * 62 + 1:8], start=(u == 0), stop=(u == 15))
                    mm.then_inc(z_h, 1)

            def out(s):
                for c in range(2):
                    n = 2 * s + c
                    pe.wait_ge(z_g, n + 1)
                    if n >= 2:
                        pe.wait_ge(z_oc, n - 1)
                    for g in range(2):
                        pe.matmul(ps[0:NCMP, 4 + c, g * HD:(g + 1) * HD], hid[:, c, s % 2, g * 63:(g + 1) * 63],
                                  w2[:, c, :], start=True, stop=False)
                        mm = pe.matmul(ps[0:NCMP, 4 + c, g * HD:(g + 1) * HD], C("ones", 1, 0, 63),
                                       b2r[0:1, c * P + g * HD:c * P + (g + 1) * HD], start=False, stop=True)
                    mm.then_inc(z_o, 1)

            hidden(0)
            for s in range(NS):
                if s + 1 < NS:
                    turn(s + 1)
                    hidden(s + 1)
                out(s)
            pe.wait_ge(z_n, 1)
            for s in range(NS):
                mm = pe.transpose(ps[:, s // 5, (s % 5) * 64:(s % 5) * 64 + 63], cko[0:63, s, 0, :], C("ident", 63, 0, 63))
            mm.then_inc(z_nt, 1)

        def cmp_act(act):
            act.wait_ge(out_s, 16 * outs[0])
            act.wait_ge(z_pe0, 1)
            act.activation(hb[:, 0:1], ps[:, 7, 0:1], ACT.Identity, bias=G("b1", 0))
            act.activation(hb[:, 1:2], ps[:, 7, 1:2], ACT.Identity, bias=G("b1", 1))
            act.drain()

            def copies(s):
                if s == 0:
                    for c in range(2):
                        for g in range(2):
                            for t in range(2):
                                ins = act.activation(xp[64 * t:64 * t + 64, 0, c, g, :],
                                                     mix[64 * g:64 * g + 64, c, t:SEQ:2], ACT.Copy)
                            ins.then_inc(z_x, 1)
                    return
                for c in range(2):
                    for g in range(2):
                        k = 4 * (s - 1) + 2 * c + g
                        act.wait_ge(z_t, k + 1)
                        if s >= 2 and c == 0 and g == 0:
                            act.wait_ge(z_h, 2 * (s - 1))
                        act.activation(xp[:, s % 2, c, g, :], ps[:, k % 2, :], ACT.Copy).then_inc(z_x, 1)

            def gelu(s):
                for c in range(2):
                    n = 2 * s + c
                    act.wait_ge(z_h, n + 1)
                    if n >= 1:
                        act.wait_ge(z_g, n)
                    act.activation(g_u[:, 0, :], ps[:, 2 + c, 0:126], ACT.Identity, bias=hb[:, c:c + 1]).then_inc(z_u, 1)
                    act.drain()
                    act.activation(g_u[:, 1, :], g_u[:, 0, :], ACT.Square).then_inc(z_hb, 1)
                    act.wait_ge(z_th, n + 1)
                    act.activation(g_u[:, 3, :], g_u[:, 2, :], ACT.Tanh, scale=float(np.sqrt(2 / np.pi))).then_inc(z_hb, 1)

            copies(0)
            for s in range(NS):
                if s + 1 < NS:
                    copies(s + 1)
                gelu(s)
                for c in range(2):
                    act.wait_ge(z_o, 2 * s + c + 1)
                    act.activation(cko[0:63, s, c, :], ps[0:NCMP, 4 + c, 0:P], ACT.Copy).then_inc(z_oc, 1)
            act.drain()
            act.activation(ckq[0:63, :, :].rearrange("p (s g) d -> p s (g d)", g=2), cko[0:63, :, 0, :], ACT.Square).then_inc(z_nc, 1)
            act.wait_ge(z_n2, 1)
            act.activation(ckr[0:63, 0, :], ckr[0:63, 1, :], ACT.Sqrt, bias=eps_c[0:63, 0:1], scale=1.0 / HD).then_inc(z_nc, 1)
            act.wait_ge(z_nt, 1)
            for s in range(1, NS):
                act.activation(ck_s[:, s - 1, 0:63], ps[:, s // 5, (s % 5) * 64:(s % 5) * 64 + 63], ACT.Copy)
                act.activation(cv_s[0:63, s - 1, :], cko[0:63, s, 1, :], ACT.Copy)
            for g in range(2):
                act.activation(ckp[:, g, 0:63], ps[64 * g:64 * g + 64, 0, 0:63], ACT.Copy)
            act.activation(cvp[0:63, :], cko[0:63, 0, 1, :], ACT.Copy)

        def cmp_dve(dve):
            for n in range(2 * NS):
                s, c = n // 2, n % 2
                dve.wait_ge(z_hb, 2 * n + 1)
                dve.tensor_scalar(g_u[:, 1, :], g_u[:, 1, :], 0.044715, 1.0, ALU.mult, ALU.add)
                dve.drain()
                dve.tensor_tensor(g_u[:, 2, :], g_u[:, 1, :], g_u[:, 0, :], ALU.mult).then_inc(z_th, 1)
                dve.wait_ge(z_hb, 2 * n + 2)
                dve.tensor_scalar(g_u[:, 3, :], g_u[:, 3, :], 1.0, 0.5, ALU.add, ALU.mult)
                dve.drain()
                if n >= 4:
                    dve.wait_ge(z_o, n - 3)
                dve.tensor_tensor(hid[:, c, s % 2, :], g_u[:, 3, :], g_u[:, 0, :], ALU.mult).then_inc(z_g, 1)
            dve.memset(ckp[:, :, :], 0.0)
            dve.memset(cvp[:, :], 0.0)
            dve.memset(cv_s[:, :, :], 0.0)
            dve.memset(ck_s[:, :, :], 0.0)
            dve.wait_ge(z_nc, 1)
            dve.tensor_reduce(ckr[0:63, 1, :], ckq[0:63, :, :], AX, ALU.add)
            dve.drain()
            dve.sem_inc(z_n2, 1)
            dve.wait_ge(z_nc, 2)
            dve.reciprocal(ckr[0:63, 0, :], ckr[0:63, 0, :])
            dve.drain()
            ck4 = cko[0:63, :, 0, :].rearrange("p s (g d) -> p s g d", g=2)
            rr = ckr[0:63, 0, :].rearrange("p (s g) -> p s g", g=2)
            dve.tensor_tensor(ck4, ck4, rr.unsqueeze(3).to_broadcast([63, NS, 2, HD]), ALU.mult)
            dve.drain()
            flat = cko[0:63, :, 0, :].rearrange("p s (g d) -> p s g d", g=2)
            dve.tensor_tensor(flat, flat, gkr[0:63, :].unsqueeze(1).unsqueeze(1).to_broadcast([63, NS, 2, HD]),
                              ALU.mult).then_inc(z_n, 1)

        q_at = [h_at]
        c2 = pack(q_at, "c2", [P, A["con2"].shape[1]])
        qs = pack(q_at, "qs", [80, 2, 6, P])
        pc = pack(q_at, "pc", [P, 6, 64])
        pcg = pack(q_at, "pcg", [P, 6, 64])
        pct = pack(q_at, "pct", [64, 2, 6, P])
        cf = pack(q_at, "cf", [P, 4, 8])
        sz = pack(q_at, "sz", [P, 72])
        im = pack(q_at, "im", [P, 3, 16])
        rk = pack(q_at, "rk", [P, 2, 256])
        mk = pack(q_at, "mk", [P, 16])
        gt = pack(q_at, "gt", [P, 9, 36])
        gt_end = q_at[0]
        pj = pack(q_at, "pj", [P, 2, SEQ])
        pt = pack(q_at, "pt", [P, 2, 8, P])
        jf = pack(q_at, "jf", [P, 2, 4])
        g_raw = rows2

        assert q_at[0] <= h_end

        def K2(name, rows=P, lo=0, n=None):
            at, r, w = _C2[name]
            return c2[0:rows, at + lo:at + (w if n is None else lo + n)]

        UN = 2 * NT
        JOBS = 12 * UN
        job = lambda n: (n // 12, (n % 12) // 2, n % 2)

        def first_key(n):
            u, z, br = job(n)
            i = u % NT
            return max(0, i - 4) if br else 0

        def nkt(n):
            return job(n)[0] % NT + 1 - first_key(n)

        D_AT, A_AT, C_AT = 9, 3, 5
        uses4, uses5 = {}, {}

        def _count():
            a = b = 0
            for ev in [("D", 0)] + [e for n in range(JOBS) for e in ((
                    [("D", n // 12 + 1)] if n % 12 == D_AT and n // 12 + 1 < UN else []) + [("J", n)])]:
                uses4[ev], uses5[ev] = a, b
                a += 1
                b += 1 if ev[0] == "D" or nkt(ev[1]) > 4 else 0
        _count()
        (j_s, j_m, j_e, j_n, j_t, j_4, j_5, j_v, j_o) = (sem(x) for x in (
            "j_s", "j_m", "j_e", "j_n", "j_t", "j_4", "j_5", "j_v", "j_o"))
        (u_q, u_s, u_x, u_e, u_k, u_mt, u_m, u_t) = (sem(x) for x in (
            "u_q", "u_s", "u_x", "u_e", "u_k", "u_mt", "u_m", "u_t"))
        ga_s, ga_t, ga_c, c2_ld = sem("ga_s"), sem("ga_t"), sem("ga_c"), sem("c2_ld")

        def gates1_act(act):
            act.wait_ge(ga_t, 1)
            act.activation(gt[:, 0:NT, :], ps[:, 6, 0:36 * NT].rearrange("p (s c) -> p s c", c=36), ACT.Copy)
            act.activation(gt[0:NB, NT, :], ps[0:NB, 7, 0:36], ACT.Copy)

        def gates1_pe(pe):
            for s in range(NT):
                pe.transpose(ps[:, 6, s * 36:(s + 1) * 36], g_raw[:, s * P:(s + 1) * P], C("ident", 36, 0, 36))
            pe.transpose(ps[0:NB, 7, 0:36], g_raw[:, SEQ:N], C("ident", 36, 0, 36)).then_inc(ga_t, 1)

        def unit(u):
            g, i = u // NT, u % NT
            return g, i, 8 * (i + 1)

        def A_act(act, u):
            g, i, w = unit(u)
            if u >= 2:
                act.wait_ge(j_s, 12 * (u - 1))
            for r in range(2):
                ins = act.activation(qs[0:64, u % 2, r::2, :], mix[64 * r:64 * r + 64, 3 * g:3 * g + 3, i * P:(i + 1) * P],
                                     ACT.Copy, scale=0.125)
            ins.then_inc(u_q, 1)

        def A_pe(pe, u):
            g, i, w = unit(u)
            pe.wait_ge(u_q, u + 1)
            if u >= 1:
                pe.wait_ge(u_m, u)
            for z in range(6):
                mm = pe.matmul(ps[:, 7, z * 64:z * 64 + w], qs[0:64, u % 2, z, :], ckp[:, g, 0:w], start=True, stop=True)
            mm.then_inc(u_s, 1)

        def A_dve(dve, u):
            g, i, w = unit(u)
            dve.wait_ge(u_s, u + 1)
            s = ps[:, 7, 0:384].rearrange("p (z n) -> p z n", z=6)
            n0 = max(0, w - 16)
            if n0:
                dve.tensor_copy(pc[:, :, 0:n0], s[:, :, 0:n0])
            dve.tensor_tensor(pc[:, :, n0:w], s[:, :, n0:w], cbias[:, 6 * g:6 * g + 6, 16 - (w - n0):16], ALU.add)
            dve.drain()
            dve.tensor_reduce(cf[:, 0, 0:6], pc[:, :, 0:w], AX, ALU.max)
            dve.drain()
            dve.tensor_tensor(pc[:, :, 0:w], pc[:, :, 0:w], cf[:, 0, 0:6].unsqueeze(2).to_broadcast([P, 6, w]),
                              ALU.subtract).then_inc(u_x, 1)

        def C_act(act, u):
            g, i, w = unit(u)
            act.wait_ge(u_x, u + 1)
            act.activation(pc[:, :, 0:w], pc[:, :, 0:w], ACT.Exp).then_inc(u_e, 1)

        def C_dve(dve, u):
            g, i, w = unit(u)
            dve.wait_ge(u_e, u + 1)
            dve.tensor_reduce(cf[:, 1, 0:6], pc[:, :, 0:w], AX, ALU.add)
            dve.drain()
            dve.reciprocal(cf[:, 2, 0:6], cf[:, 1, 0:6])
            dve.drain()
            if i == 0:
                dve.tensor_scalar(cf[:, 2, 0:6], cf[:, 2, 0:6], K2("seen")[:, 0:1], None, ALU.mult)
                dve.drain()
            dve.tensor_tensor(pc[:, :, 0:w], pc[:, :, 0:w], cf[:, 2, 0:6].unsqueeze(2).to_broadcast([P, 6, w]), ALU.mult)
            dve.drain()
            dve.scalar_tensor_tensor(out=pc[:, :, 0:w], in0=pc[:, :, 0:w], scalar=TINY, in1=pc[:, :, 0:w],
                                     op0=ALU.is_ge, op1=ALU.mult)
            dve.memset(sz[:, :], 0.0)
            dve.drain()
            if u >= 1:
                dve.wait_ge(u_t, u)
            dve.tensor_tensor(pcg[:, :, 0:w], pc[:, :, 0:w],
                              gt[:, i, 6 * g:6 * g + 6].unsqueeze(2).to_broadcast([P, 6, w]), ALU.mult)
            dve.tensor_reduce(sz[:, 4:4 + w], pc[:, :, 0:w].rearrange("p z n -> p n z"), AX, ALU.add)
            dve.drain()
            dve.tensor_reduce(im[:, 0, :], sz[:, 4:68].rearrange("p (j r) -> p j r", r=4)[:, :, 0:3], AX, ALU.add)
            dve.drain()
            dve.scalar_tensor_tensor(out=im[:, 1, :], in0=im[:, 0, :], scalar=2.0, in1=sz[:, 7:71:4], op0=ALU.mult, op1=ALU.add)
            dve.drain()
            dve.tensor_tensor(im[:, 0, :], im[:, 1, :], sz[:, 3:67:4], ALU.add)
            dve.drain()
            dve.tensor_tensor(im[:, 1, :], im[:, 0, :], K2("valid", P, 16 * i, 16), ALU.mult)
            dve.drain()
            dve.tensor_tensor(im[:, 2, :], im[:, 1, :], K2("forced", P, 16 * i, 16), ALU.add)
            dve.drain()
            sj = im[:, 2, :].unsqueeze(2).to_broadcast([P, 16, 16])
            si = im[:, 2, :].unsqueeze(1).to_broadcast([P, 16, 16])
            r0 = rk[:, 0, :].rearrange("p (j i) -> p j i", j=16)
            r1 = rk[:, 1, :].rearrange("p (j i) -> p j i", j=16)
            dve.tensor_tensor(r0, si, sj, ALU.is_equal)
            dve.tensor_tensor(r1, si, sj, ALU.is_gt)
            dve.drain()
            dve.tensor_tensor(rk[:, 0, :], rk[:, 0, :], K2("before"), ALU.mult)
            dve.drain()
            dve.tensor_tensor(rk[:, 1, :], rk[:, 1, :], rk[:, 0, :], ALU.add)
            dve.drain()
            dve.tensor_reduce(im[:, 0, :], r1, AX, ALU.add)
            dve.drain()
            dve.tensor_scalar(mk[:, :], im[:, 0, :], 7.5, NEG, ALU.is_gt, ALU.mult).then_inc(u_k, 1)

        def D_pe(pe, u):
            g, i, w = unit(u)
            pe.wait_ge(u_k, u + 1)
            pe.transpose(ps[0:16, 7, 384:512], mk[:, :], C("ident")).then_inc(u_mt, 1)
            if uses4[("D", u)]:
                pe.wait_ge(j_4, uses4[("D", u)])
            if uses5[("D", u)]:
                pe.wait_ge(j_5, uses5[("D", u)])
            for z in range(6):
                mm = pe.transpose(ps[0:w, 4 + z // 4, (z % 4) * P:(z % 4 + 1) * P], pcg[:, z, 0:w], C("ident"))
            mm.then_inc(u_t, 1)

        def D_act(act, u):
            g, i, w = unit(u)
            act.wait_ge(u_mt, u + 1)
            act.activation(qs[64:80, u % 2, :, :], ps[0:16, 7, 384:512].unsqueeze(1).to_broadcast([16, 6, P]),
                           ACT.Copy).then_inc(u_m, 1)
            act.wait_ge(u_t, u + 1)
            act.activation(pct[0:w, u % 2, 0:4, :], ps[0:w, 4, :].rearrange("p (z t) -> p z t", z=4), ACT.Copy).then_inc(j_4, 1)

        def D_dve(dve, u):
            g, i, w = unit(u)
            dve.wait_ge(u_t, u + 1)
            dve.tensor_copy(pct[0:w, u % 2, 4:6, :], ps[0:w, 5, 0:256].rearrange("p (z t) -> p z t", z=2)).then_inc(j_5, 1)

        def nsa_pe(pe):
            def scores(n):
                u, z, br = job(n)
                g, i, _ = unit(u)
                if n >= 2:
                    pe.wait_ge(j_e, n - 1)
                pe.wait_ge(u_m, u + 1)
                r = 64 if br else 80
                k0 = first_key(n) * P
                nk = nkt(n) * P
                for c in range(0, nk, 512):
                    w = min(512, nk - c)
                    mm = pe.matmul(ps[:, 2 * (n % 2) + c // 512, 0:w], qs[0:r, u % 2, z, :],
                                   kk[0:r, br, g, k0 + c:k0 + c + w], start=True, stop=True)
                mm.then_inc(j_s, 1)

            def turn(n):
                pe.wait_ge(j_n, n + 1)
                pe.wait_ge(j_4, uses4[("J", n)])
                if nkt(n) > 4:
                    pe.wait_ge(j_5, uses5[("J", n)])
                for t in range(nkt(n)):
                    mm = pe.transpose(ps[:, 4 + t // 4, (t % 4) * P:(t % 4 + 1) * P], pj[:, n % 2, t * P:(t + 1) * P], C("ident"))
                mm.then_inc(j_t, 1)

            def values(n):
                u, z, br = job(n)
                g, i, w = unit(u)
                p0 = 64 * (z % 2)
                o = ps[p0:p0 + 64, 6, (z // 2) * P:(z // 2 + 1) * P]
                if n % 12 == 0 and u:
                    pe.wait_ge(j_o, u)
                if n % 12 == 0:
                    pe.wait_ge(j_4, uses4[("D", u)] + 1)
                    pe.wait_ge(j_5, uses5[("D", u)] + 1)
                if not br:
                    pe.matmul(o, cvp[0:w, g * HD:(g + 1) * HD], pct[0:w, u % 2, z, :], start=True, stop=False,
                              skip_group_check=True)
                pe.wait_ge(j_4, uses4[("J", n)] + 1)
                if nkt(n) > 4:
                    pe.wait_ge(j_5, uses5[("J", n)] + 1)
                for t in range(nkt(n)):
                    mm = pe.matmul(o, vv[:, br, first_key(n) + t, g * HD:(g + 1) * HD], pt[:, n % 2, t, :],
                                   start=False, stop=(br == 1 and t == nkt(n) - 1), skip_group_check=True)
                mm.then_inc(j_v, 1)

            A_pe(pe, 0)
            D_pe(pe, 0)
            scores(0)
            scores(1)
            for n in range(JOBS):
                u = n // 12 + 1
                if n + 2 < JOBS:
                    scores(n + 2)
                if u < UN and n % 12 == D_AT:
                    D_pe(pe, u)
                turn(n)
                if n:
                    values(n - 1)
                if u < UN and n % 12 == A_AT:
                    A_pe(pe, u)
            values(JOBS - 1)

        def nsa_act(act):
            def exps(n):
                act.wait_ge(j_m, n + 1)
                if n >= 2:
                    act.wait_ge(j_t, n - 1)
                nk = nkt(n) * P
                src = ps[:, 2 * (n % 2):2 * (n % 2) + 2, :].rearrange("p a k -> p (a k)")[:, 0:nk]
                act.activation(pj[:, n % 2, 0:nk], src, ACT.Exp, bias=jf[:, n % 2, 0:1],
                               accum_out=jf[:, n % 2, 1:2]).then_inc(j_e, 1)

            A_act(act, 0)
            C_act(act, 0)
            D_act(act, 0)
            def turned(n):
                act.wait_ge(j_t, n + 1)
                if n >= 2:
                    act.wait_ge(j_v, n - 1)
                m = min(4, nkt(n))
                act.activation(pt[:, n % 2, 0:m, :], ps[:, 4, 0:m * P].rearrange("p (m t) -> p m t", m=m),
                               ACT.Copy).then_inc(j_4, 1)

            def heads(u):
                g, i, _ = unit(u)
                act.wait_ge(j_v, 12 * (u + 1))
                act.activation(mix[:, 3 * g:3 * g + 3, i * P:(i + 1) * P],
                               ps[:, 6, 0:384].rearrange("p (j t) -> p j t", j=3), ACT.Copy).then_inc(j_o, 1)

            exps(0)
            for n in range(JOBS):
                u = n // 12 + 1
                if n:
                    turned(n - 1)
                if n % 12 == 1 and n > 12:
                    heads(u - 2)
                if u < UN and n % 12 == D_AT:
                    D_act(act, u)
                if n + 1 < JOBS:
                    exps(n + 1)
                if u < UN:
                    if n % 12 == A_AT - 1:
                        A_act(act, u)
                    if n % 12 == C_AT:
                        C_act(act, u)
            turned(JOBS - 1)
            heads(UN - 1)

        def nsa_dve(dve):
            def maxes(n):
                u, z, br = job(n)
                g, i, _ = unit(u)
                dve.wait_ge(j_s, n + 1)
                nk = nkt(n) * P
                s = ps[:, 2 * (n % 2):2 * (n % 2) + 2, :].rearrange("p a k -> p (a k)")
                w = min(256, nk)
                dve.tensor_tensor(s[:, nk - w:nk], s[:, nk - w:nk], bias[:, 6 * g + z, 256 - w:256], ALU.add)
                if br and i >= 4:
                    dve.tensor_tensor(s[:, 0:P], s[:, 0:P], K2("edge"), ALU.add)
                dve.drain()
                dve.tensor_reduce(jf[:, n % 2, 0:1], s[:, 0:nk], AX, ALU.max, negate=True).then_inc(j_m, 1)

            def norm(n):
                u, z, br = job(n)
                g, i, _ = unit(u)
                nk = nkt(n) * P
                dve.wait_ge(j_e, n + 1)
                dve.reciprocal(jf[:, n % 2, 2:3], jf[:, n % 2, 1:2])
                dve.drain()
                dve.tensor_scalar(pj[:, n % 2, 0:nk], pj[:, n % 2, 0:nk], jf[:, n % 2, 2:3],
                                  gt[:, i, 12 * (1 + br) + 6 * g + z:12 * (1 + br) + 6 * g + z + 1],
                                  ALU.mult, ALU.mult).then_inc(j_n, 1)

            A_dve(dve, 0)
            C_dve(dve, 0)
            D_dve(dve, 0)
            def turned(n):
                if nkt(n) > 4:
                    dve.wait_ge(j_t, n + 1)
                    if n >= 2:
                        dve.wait_ge(j_v, n - 1)
                    m = nkt(n) - 4
                    dve.tensor_copy(pt[:, n % 2, 4:4 + m, :],
                                    ps[:, 5, 0:m * P].rearrange("p (m t) -> p m t", m=m)).then_inc(j_5, 1)

            maxes(0)
            maxes(1)
            for n in range(JOBS):
                u = n // 12 + 1
                norm(n)
                if n:
                    turned(n - 1)
                if u < UN and n % 12 == D_AT:
                    D_dve(dve, u)
                if n + 2 < JOBS:
                    maxes(n + 2)
                if u < UN:
                    if n % 12 == A_AT:
                        A_dve(dve, u)
                    if n % 12 == C_AT:
                        C_dve(dve, u)
            turned(JOBS - 1)

        R = NB * NH
        s_at = [h_at + ((4 * A["con2"].shape[1] + 31) // 32 * 32)]
        gt2 = pack(s_at, "gt2", [NB, 36])
        vs_at = s_at[0]
        s_at[0] += 4 * NB * 8 * P
        qz12 = pack(s_at, "qz12", [P, NB, R])
        tabr = pack(s_at, "tabr", [33, R])
        ohs = pack(s_at, "ohs", [33, 256])
        pt2 = pack(s_at, "pt2", [1, 64], I32)
        sp_ = pack(s_at, "sp_", [R, 1602])
        spt = pack(s_at, "spt", [P, 12, R])
        spc = pack(s_at, "spc", [64, R])
        pnd = pack(s_at, "pnd", [NB, 2, R])
        vnw = pack(s_at, "vnw", [NB, 2, P])
        dgn = pack(s_at, "dgn", [R, 2, R])
        sfm = pack(s_at, "sfm", [R, 3, 8])
        gts = pack(s_at, "gts", [R, 40])
        szs = pack(s_at, "szs", [R, 72])
        ims = pack(s_at, "ims", [R, 4, 17])
        rks = pack(s_at, "rks", [R, 2, 289])
        pass
        assert s_at[0] <= h_end
        t_at = [a2]
        vs_w = pack(t_at, "vs_w", [P, NB, 4, P])
        both = place("both", [P, (arena_end - vs_at) // 4], at=vs_at)

        def v_of(b, pg):
            return (b * 8 + pg) * P

        def k_of(b, pg):
            return (w_hi_at - vs_at) // 4 + (b % 2) * SEQ + pg * P

        def page_to(b, pg):
            to_v, to_k = v_of(b, pg), k_of(b, pg)
            return both[:, to_v:to_v + 2 * (to_k - to_v)].rearrange("p (a s) -> p a s", a=2)[:, :, 0:P]

        kTw = pack(t_at, "kTw", [P, 2, 512])
        assert t_at[0] <= a2 + 4 * (4 * SEQ + 2 * NT * P + NH * 256)
        y_ld, y_k, y_v, y_w = sem("y_ld"), [sem("y_k0"), sem("y_k1")], sem("y_v"), [sem("y_w0"), sem("y_w1")]
        y_q, y_s, y_c, y_ce, y_g, y_gs, y_m, y_e, y_p, y_n, y_nc, y_x = (sem(x) for x in (
            "y_q", "y_s", "y_c", "y_ce", "y_g", "y_gs", "y_m", "y_e", "y_p", "y_n", "y_nc", "y_x"))

        def snsa_sp(sp):
            sp.dma_start(pt2[:, :], A["pt"]).then_inc(y_ld, 16)
            sp.wait_ge(y_ld, 16)
            sp.dma_start(tabr[0:32, :].rearrange("p (b h) -> p b h", b=NB), A["table8"]).then_inc(y_ld, 16)
            sp.dma_start(ohs[:, :], A["ohs"]).then_inc(y_ld, 16)
            for b in range(NB):
                if b >= 2:
                    sp.wait_ge(y_s, b - 1)
                for pg in range(8):
                    v = sp.value_load(pt2[0:1, b * 8 + pg:b * 8 + pg + 1], min_val=0, max_val=A["slc"].shape[0] - 1)
                    sp.dma_start(page_to(b, pg), A["slc"][v]).then_inc(y_k[b % 2], 16)
                sp.dma_start(kTw[:, b % 2, :], A["win_k"][b]).then_inc(y_w[b % 2], 16)
                sp.dma_start(vs_w[:, b, :, :], A["win_v"][b]).then_inc(y_v, 16)

        def snsa_pe(pe):
            pe.wait_ge(y_ld, 48)
            pe.wait_ge(y_q, 1)
            for b in range(NB):
                pe.matmul(ps[0:R, 0, 0:64], qz12[:, b, :], ck_s[:, b, :], start=(b == 0), stop=False)
            pe.matmul(ps[0:R, 0, 0:64], tabr[:, :], ohs[:, 0:64], start=False, stop=True)
            for br in range(2):
                for b in range(NB):
                    pe.matmul(ps[0:R, 0, 64 + br:65 + br], qz12[:, b, :], kvn[:, 2 + 2 * br, b:b + 1], start=(b == 0), stop=False)
                mm = pe.matmul(ps[0:R, 0, 64 + br:65 + br], tabr[:, :], ohs[:, 192:193], start=False, stop=True)
            mm.then_inc(y_c, 1)
            pe.matmul(ps[0:R, 7, 0:36], K2("b_rows", NB), gt2[:, :], start=True, stop=True)
            for br in range(2):
                mm = pe.transpose(ps[0:NB, 7, 64 + br * P:64 + (br + 1) * P], kvn[:, 3 + 2 * br, :], C("ident"))
            mm.then_inc(y_g, 1)
            for b in range(NB):
                pe.wait_ge(y_k[b % 2], 16 * 8 * (b // 2 + 1))
                pe.wait_ge(y_w[b % 2], 16 * (b // 2 + 1))
                last = b == NB - 1
                pe.matmul(ps[0:R, 1, :], qz12[:, b, :], both[:, k_of(b, 0):k_of(b, 4)], start=(b == 0), stop=last)
                pe.matmul(ps[0:R, 2, :], qz12[:, b, :], both[:, k_of(b, 4):k_of(b, 4) + 512], start=(b == 0), stop=False)
                pe.matmul(ps[0:R, 3, :], qz12[:, b, :], kTw[:, b % 2, :], start=(b == 0), stop=False).then_inc(y_s, 1)
            pe.matmul(ps[0:R, 2, 384:512], tabr[:, :], ohs[:, 64:192], start=False, stop=True)
            pe.matmul(ps[0:R, 3, 384:512], tabr[:, :], ohs[:, 64:192], start=False, stop=True).then_inc(y_s, 1)
            pe.wait_ge(y_ce, 1)
            pe.matmul(ps[0:R, 7, 0:64], K2("groups", R), sp_[:, 0:64], start=True, stop=True).then_inc(y_gs, 1)
            pe.wait_ge(y_p, 1)
            pe.transpose(ps[0:64, 4, 0:R], sp_[:, 0:64], C("ident", R, 0, R))
            for br in range(2):
                pe.matmul(ps[0:NB, 4, 128 + R * br:128 + R * (br + 1)], K2("row_b", R), dgn[:, br, :], start=True, stop=True)
            for t in range(12):
                c0 = 64 + t * P if t < 8 else 1089 + (t - 8) * P
                mm = pe.transpose(ps[:, 5 + t // 4, (t % 4) * R:(t % 4 + 1) * R], sp_[:, c0:c0 + P], C("ident", R, 0, R))
            mm.then_inc(y_n, 1)
            pe.wait_ge(y_nc, 1)
            pe.wait_ge(y_v, 16 * NB)
            for b in range(NB):
                o = ps[:, 0, b * NH:(b + 1) * NH]
                cols = slice(b * NH, (b + 1) * NH)
                pe.matmul(o, cv_s[:, b, :], spc[:, cols], start=True, stop=False)
                for br in range(2):
                    pe.matmul(o, vnw[:, br, :], pnd[:, br, cols], start=False, stop=False)
                for t in range(12):
                    v = both[:, v_of(b, t):v_of(b, t) + P] if t < 8 else vs_w[:, b, t - 8, :]
                    mm = pe.matmul(o, v, spt[:, t, cols], start=False, stop=(t == 11))
            mm.then_inc(y_x, 1)

        def snsa_act(act):
            act.wait_ge(y_q, 1)
            act.wait_ge(y_g, 1)
            act.activation(gts[:, 0:36], ps[0:R, 7, 0:36], ACT.Copy)
            act.activation(vnw[:, :, :], ps[0:NB, 7, 64:320].rearrange("p (a d) -> p a d", a=2), ACT.Copy).then_inc(y_gs, 1)
            act.wait_ge(y_m, 1)
            act.activation(sp_[:, 0:64], sp_[:, 0:64], ACT.Exp, bias=sfm[:, 0, 0:1],
                           accum_out=sfm[:, 1, 0:1]).then_inc(y_e, 1)
            for br in range(2):
                act.wait_ge(y_m, 2 + br)
                c0, n = (64, 1025) if br == 0 else (1090, 512)
                act.activation(sp_[:, c0:c0 + n], sp_[:, c0:c0 + n], ACT.Exp, bias=sfm[:, 0, 1 + br:2 + br],
                               accum_out=sfm[:, 1, 1 + br:2 + br]).then_inc(y_e, 1)
            act.wait_ge(y_n, 1)
            for q in range(3):
                act.activation(spt[:, 4 * q:4 * q + 4, :], ps[:, 5 + q, 0:4 * R].rearrange("p (t c) -> p t c", t=4), ACT.Copy)
            act.activation(spc[:, :], ps[0:64, 4, 0:R], ACT.Copy)
            act.activation(pnd[:, :, :], ps[0:NB, 4, 128:128 + 2 * R].rearrange("p (a c) -> p a c", a=2), ACT.Copy).then_inc(y_nc, 1)
            act.wait_ge(y_x, 1)
            for h in range(NH):
                p0, g = 64 * (h % 2), h // 6
                act.activation(mix[p0:p0 + 64, h // 2, SEQ:N], ps[64 * g:64 * g + 64, 0, h:h + NH * (NB - 1) + 1:NH], ACT.Copy)

        def snsa_dve(dve):
            dve.memset(qz12[:, :, :], 0.0)
            dve.memset(tabr[32:33, :], NEG)
            dve.memset(szs[:, :], 0.0)
            dve.drain()
            qf = qz12[:, :, :].rearrange("p b c -> p (b c)")
            for h in range(NH):
                p0, g = 64 * (h % 2), h // 6
                dve.tensor_scalar(qf[64 * g:64 * g + 64, h:h + (R + NH) * (NB - 1) + 1:R + NH],
                                  mix[p0:p0 + 64, h // 2, SEQ:N], 0.125, None, ALU.mult)
            dve.drain()
            dve.sem_inc(y_q, 1)
            dve.wait_ge(y_c, 1)
            dve.tensor_copy(sp_[:, 0:64], ps[0:R, 0, 0:64])
            dve.tensor_copy(sp_[:, 1088:1089], ps[0:R, 0, 64:65])
            dve.tensor_copy(sp_[:, 1601:1602], ps[0:R, 0, 65:66])
            dve.drain()
            dve.tensor_reduce(sfm[:, 0, 0:1], sp_[:, 0:64], AX, ALU.max, negate=True).then_inc(y_m, 1)

            dve.wait_ge(y_e, 1)
            dve.reciprocal(sfm[:, 2, 0:1], sfm[:, 1, 0:1])
            dve.drain()
            dve.tensor_scalar(sp_[:, 0:64], sp_[:, 0:64], sfm[:, 2, 0:1], None, ALU.mult)
            dve.drain()
            dve.scalar_tensor_tensor(out=sp_[:, 0:64], in0=sp_[:, 0:64], scalar=TINY, in1=sp_[:, 0:64],
                                     op0=ALU.is_ge, op1=ALU.mult)
            dve.drain()
            dve.sem_inc(y_ce, 1)
            dve.wait_ge(y_gs, 2)
            dve.tensor_copy(szs[:, 4:67], ps[0:R, 7, 0:63])
            dve.tensor_tensor(gts[:, 0:36], gts[:, 0:36], K2("h_pick", R), ALU.mult)
            dve.memset(ims[:, :, :], 0.0)
            dve.drain()
            dve.tensor_reduce(gts[:, 36:39], gts[:, 0:36].rearrange("p (a h) -> p a h", a=3), AX, ALU.add)
            dve.tensor_reduce(ims[:, 0, 0:16], szs[:, 4:68].rearrange("p (j r) -> p j r", r=4)[:, :, 0:3], AX, ALU.add)
            dve.drain()
            dve.scalar_tensor_tensor(out=ims[:, 1, 0:16], in0=ims[:, 0, 0:16], scalar=2.0, in1=szs[:, 7:71:4],
                                     op0=ALU.mult, op1=ALU.add)
            dve.drain()
            dve.tensor_tensor(ims[:, 0, 0:16], ims[:, 1, 0:16], szs[:, 3:67:4], ALU.add)
            dve.drain()
            dve.tensor_tensor(ims[:, 1, :], ims[:, 0, :], K2("valid_s", R), ALU.mult)
            dve.drain()
            dve.tensor_tensor(ims[:, 2, :], ims[:, 1, :], K2("forced_s", R), ALU.add)
            dve.drain()
            sj = ims[:, 2, :].unsqueeze(2).to_broadcast([R, 17, 17])
            si = ims[:, 2, :].unsqueeze(1).to_broadcast([R, 17, 17])
            r0 = rks[:, 0, :].rearrange("p (j i) -> p j i", j=17)
            r1 = rks[:, 1, :].rearrange("p (j i) -> p j i", j=17)
            dve.tensor_tensor(r0, si, sj, ALU.is_equal)
            dve.tensor_tensor(r1, si, sj, ALU.is_gt)
            dve.drain()
            dve.tensor_tensor(rks[:, 0, :], rks[:, 0, :], K2("before_s", R), ALU.mult)
            dve.drain()
            dve.tensor_tensor(rks[:, 1, :], rks[:, 1, :], rks[:, 0, :], ALU.add)
            dve.drain()
            dve.tensor_reduce(ims[:, 0, :], r1, AX, ALU.add)
            dve.drain()
            dve.tensor_scalar(ims[:, 3, :], ims[:, 0, :], 7.5, NEG, ALU.is_gt, ALU.mult)
            dve.drain()
            dve.wait_ge(y_s, NB + 1)
            for half in range(2):
                dve.tensor_tensor(sp_[:, 64 + 512 * half:576 + 512 * half].rearrange("p (j k) -> p j k", k=64),
                                  ps[0:R, 1 + half, :].rearrange("p (j k) -> p j k", k=64),
                                  ims[:, 3, 8 * half:8 * half + 8].unsqueeze(2).to_broadcast([R, 8, 64]), ALU.add)
            dve.tensor_tensor(sp_[:, 1088:1089], sp_[:, 1088:1089], ims[:, 3, 16:17], ALU.add)
            dve.drain()
            dve.tensor_reduce(sfm[:, 0, 1:2], sp_[:, 64:1089], AX, ALU.max, negate=True).then_inc(y_m, 1)
            dve.tensor_copy(sp_[:, 1089:1601], ps[0:R, 3, :])
            dve.drain()
            dve.tensor_reduce(sfm[:, 0, 2:3], sp_[:, 1090:1602], AX, ALU.max, negate=True).then_inc(y_m, 1)
            dve.memset(sp_[:, 1089:1090], 0.0)
            dve.wait_ge(y_e, 3)
            dve.reciprocal(sfm[:, 2, 1:3], sfm[:, 1, 1:3])
            dve.drain()
            dve.tensor_scalar(sp_[:, 0:64], sp_[:, 0:64], gts[:, 36:37], None, ALU.mult)
            for br, (c0, n) in enumerate(((64, 1025), (1090, 512))):
                dve.tensor_scalar(sp_[:, c0:c0 + n], sp_[:, c0:c0 + n], sfm[:, 2, 1 + br:2 + br], gts[:, 37 + br:38 + br],
                                  ALU.mult, ALU.mult)
            dve.drain()
            for br, c0 in enumerate((1088, 1601)):
                dve.tensor_scalar(dgn[:, br, :], C("ident", R, 0, R), sp_[:, c0:c0 + 1], None, ALU.mult)
            dve.drain()
            dve.sem_inc(y_p, 1)

        hb_sq = place("hb_sq", [P, 2, N], at=h_end - 16 * N)
        hb_rt = place("hb_rt", [P, 2, N], at=h_end - 8 * N)
        assert gt_end <= h_end - 16 * N

        def projb_act(act):
            def evac(i, T, slot, j):
                act.wait_ge(tile_done, T + 1)
                if isinstance(i, int) and i == 8:
                    act.activation(three(rows2[:, :]), ps[0:36, 3 * slot:3 * slot + 3, 0:CH], ACT.Sigmoid,
                                   bias=G("b_gate", 0, 36)).then_inc(tile_free, 1)
                else:
                    act.activation(three(mix[:, i, :]), acc(slot), ACT.Copy).then_inc(tile_free, 1)
            seg_act(act, "b_q", evac, chain=False)

        sw_o = sem("sw_o")
        block = ctx.enter_context(nc.Block())

        @block.sync
        def _(sp):
            mem_sp(sp)
            for name in ("a_v", "a_q", "a_m", "a_g", "a_k"):
                load_seg(sp, name)
            sp.wait_ge(fence_s, 3 * 2)
            sp.dma_start(sm_in[:, :], A["m0"]).then_inc(ml_ld, 16)
            sp.wait_ge(fence_s, 3 * 4)
            samples_sp(sp)
            sp.wait_ge(fence_s, 3 * 5)
            load_seg(sp, "a_o")
            sp.wait_ge(fence_s, 3 * 6)
            mem_load(sp, 0)
            load_seg(sp, "out0")
            for q in range(3):
                load_seg(sp, f"gu0{q}")
                load_seg(sp, f"dn0{q}")
            load_seg(sp, "kv")
            sp.wait_ge(fence_s, 3 * 10)
            bias_sp(sp)
            sp.wait_ge(fence_s, 3 * 12)
            cmp_sp(sp)
            load_seg(sp, "b_q")
            sp.wait_ge(fence_s, 3 * 14)
            sp.dma_start(c2[:, :], A["con2"]).then_inc(c2_ld, 16)
            sp.wait_ge(fence_s, 3 * 16)
            snsa_sp(sp)
            sp.wait_ge(fence_s, 3 * 17)
            mem_load(sp, 1)
            load_seg(sp, "out1")
            for q in range(3):
                load_seg(sp, f"gu1{q}")
                load_seg(sp, f"dn1{q}")
            sp.dma_start(O["o_win"], A["win"].rearrange("b r c -> b (r c)")).then_inc(sw_o, 16)
            sp.wait_ge(fence_s, 3 * 20)
            sp.dma_start(O["o_y"], xT[:, :, :]).then_inc(sw_o, 16)
            sp.wait_ge(sw_o, 32)
        @block.scalar
        def _(act):
            mem_act(act)
            fence(act, 1)
            act.wait_ge(ld, 32)
            norm_act(act, 0, squares=True)
            proj_a_act(act)
            fence(act, 2)
            gates_act(act)
            mlstm_act(act)
            fence(act, 3)
            state_act(act)
            fence(act, 4)
            samples_act(act)
            fence(act, 5)
            ogate_act(act)
            fence(act, 6)
            hnorm_act(act, lambda t: mix[:, 6 + t, :], 2, CH, 3, hq_sq, hq_rt)
            fence(act, 7)
            attend_act(act, 0)
            fence(act, 8)
            split_act(act, 8, mix, N)
            fence(act, 9)
            sum_x(act, "out0", 1, first=True)
            norm_act(act, 1)
            ffn_act(act, 0)
            norm_act(act, 2)
            kvproj_act(act)
            fence(act, 10)
            bias_act(act)
            fence(act, 11)
            keys_act(act)
            fence(act, 12)
            cmp_act(act)
            fence(act, 13)
            norm_act(act, 3, squares=True, first="b_q")
            projb_act(act)
            fence(act, 14)
            gates1_act(act)
            hnorm_act(act, lambda t: mix[:, t, :], 8, CH, 3, hb_sq, hb_rt)
            fence(act, 15)
            act.wait_ge(c2_ld, 16)
            nsa_act(act)
            act.drain()
            act.activation(gt2[:, :], gt[0:NB, NT, :], ACT.Copy)
            fence(act, 16)
            snsa_act(act)
            fence(act, 17)
            attend_act(act, 1)
            fence(act, 18)
            split_act(act, 16, mix, N)
            fence(act, 19)
            sum_x(act, "out1", 4, first=True)
            norm_act(act, 4)
            ffn_act(act, 1)
            fence(act, 20)

        @block.vector
        def _(dve):
            mem_dve(dve)
            fence(dve, 1)
            dve.wait_ge(ld, 32)
            norm_dve(dve, 0, "g_mix0", squares=True)
            proj_a_dve(dve)
            fence(dve, 2)
            gates_dve(dve)
            mlstm_dve(dve)
            fence(dve, 3)
            state_dve(dve)
            fence(dve, 4)
            samples_dve(dve)
            fence(dve, 5)
            ogate_dve(dve)
            fence(dve, 6)
            hnorm_dve(dve, lambda t: mix[:, 6 + t, :], lambda t: mix[:, 6 + t, :], 2, N, lambda t: G("g_mem_q", 0), hq_rt)
            fence(dve, 7)
            attend_dve(dve, 0)
            fence(dve, 8)
            split_dve(dve, 8, mix, N)
            fence(dve, 9)
            add_x(dve, "out0", first=True, norm=1)
            norm_dve(dve, 1, "g_ffn0")
            ffn_dve(dve, 0)
            norm_dve(dve, 2, "g_kv")
            seg_dve(dve, "kv", None, chain=False)
            fence(dve, 10)
            bias_dve(dve)
            fence(dve, 11)
            keys_dve(dve)
            fence(dve, 12)
            cmp_dve(dve)
            fence(dve, 13)
            norm_dve(dve, 3, "g_mix1", squares=True, first="b_q")
            seg_dve(dve, "b_q", None, chain=False)
            fence(dve, 14)
            hnorm_dve(dve, lambda t: mix[:, t, :], lambda t: mix[:, t, :], 8, N,
                      lambda t: G("g_q") if t < 6 else G("g_mem_q", 1), hb_rt)
            fence(dve, 15)
            dve.wait_ge(c2_ld, 16)
            nsa_dve(dve)
            fence(dve, 16)
            snsa_dve(dve)
            fence(dve, 17)
            attend_dve(dve, 1)
            fence(dve, 18)
            split_dve(dve, 16, mix, N)
            fence(dve, 19)
            add_x(dve, "out1", first=True, norm=4)
            norm_dve(dve, 4, "g_ffn1")
            ffn_dve(dve, 1)
            fence(dve, 20)

        @block.tensor
        def _(pe):
            mem_pe(pe)
            fence(pe, 1)
            norm_pe(pe, 0)
            proj_a_pe(pe)
            fence(pe, 2)
            gates_pe(pe)
            mlstm_pe(pe)
            fence(pe, 3)
            state_pe(pe)
            fence(pe, 4)
            samples_pe(pe)
            fence(pe, 5)
            seg_pe(pe, "a_o")
            fence(pe, 6)
            hnorm_pe(pe, 2, CH, 3, hq_sq)
            fence(pe, 7)
            attend_pe(pe, 0)
            fence(pe, 8)
            fence(pe, 9)
            seg_pe(pe, "out0")
            norm_pe(pe, 1)
            ffn_pe(pe, 0)
            norm_pe(pe, 2)
            seg_pe(pe, "kv", ready=normed(2))
            fence(pe, 10)
            bias_pe(pe)
            fence(pe, 11)
            keys_pe(pe)
            fence(pe, 12)
            cmp_pe(pe)
            fence(pe, 13)
            norm_pe(pe, 3)
            seg_pe(pe, "b_q", ready=normed(3))
            fence(pe, 14)
            gates1_pe(pe)
            hnorm_pe(pe, 8, CH, 3, hb_sq)
            fence(pe, 15)
            pe.wait_ge(c2_ld, 16)
            nsa_pe(pe)
            fence(pe, 16)
            snsa_pe(pe)
            fence(pe, 17)
            attend_pe(pe, 1)
            fence(pe, 18)
            fence(pe, 19)
            seg_pe(pe, "out1")
            norm_pe(pe, 4)
            ffn_pe(pe, 1)
            fence(pe, 20)


_G = {}


def lay_gains(x):
    cols, at = [], 0

    def put(name, a):
        nonlocal at
        full = np.zeros((P, a.shape[1]), np.float32)
        full[:a.shape[0]] = a
        _G[name] = at
        cols.append(full)
        at += a.shape[1]
    for l in range(2):
        put(f"g_mix{l}", x["g_mix"][l].reshape(KC, P).T)
        put(f"g_ffn{l}", x["g_ffn"][l].reshape(KC, P).T)
    put("g_kv", x["g_kv"].reshape(KC, P).T)
    gh = x["g_hnorm"][0]
    put("g_hb", np.stack([gh[:P], gh[64:]], 1))
    put("g_hs", np.stack([gh[P:], gh[:64]], 1))
    twice = lambda a: np.concatenate([a.reshape(1, -1), a.reshape(1, -1)], 1).T
    for l in range(2):
        put(f"g_mem_k{l}", twice(x["g_mem_k"][l]))
    _G["g_mem_k"] = _G["g_mem_k0"]
    for l in range(2):
        put(f"g_mem_q{l}", twice(x["g_mem_q"][l]))
    _G["g_mem_q"] = _G["g_mem_q0"]
    put("g_q", twice(x["g_q"][0]))
    put("g_k_slc", twice(x["g_k_slc"]))
    put("g_k_win", twice(x["g_k_win"]))
    b = np.zeros((36, 1), np.float32)
    b[0:4, 0] = x["b_if"][0, :4]
    b[32:36, 0] = x["b_if"][0, 4:]
    put("b_if", b)
    put("b_gate", x["b_gate"].reshape(36, 1))
    put("b1", x["cmp_b1"].T)
    return np.concatenate(cols, 1)


def lay(w, tiles, kk=KC):
    return np.ascontiguousarray(w.reshape(kk, P, tiles, P).transpose(2, 1, 0, 3).reshape(tiles, P, kk * P))


def pad(w, n):
    out = np.zeros((w.shape[0], n), np.float32)
    out[:, :w.shape[1]] = w
    return out


def lay_inputs(x):
    d = {}
    d["con"] = constants()
    d["gain"] = lay_gains(x)
    tok = np.concatenate([x["x_prompt"][0], x["x_sample"][:, 0]], 0)
    d["xT"] = tok.T.reshape(KC, P, N).transpose(1, 0, 2)
    d["memT"] = x["mem_prompt"][0].T.reshape(KC, P, MEM).transpose(1, 0, 2)
    d["w_mem"] = np.concatenate([lay(x["w_mem_kv"][l], 4) for l in range(2)])
    wa = x["w_in_a"][0]
    g = np.zeros((DM, P), np.float32)
    g[:, 0:4] = wa[:, 4 * MIX:4 * MIX + 4]
    g[:, 32:36] = wa[:, 4 * MIX + 4:4 * MIX + 8]
    d["w_a"] = np.concatenate([lay(wa[:, 2 * MIX:3 * MIX], 6), lay(wa[:, :MIX], 6), lay(wa[:, 4 * MIX + 8:], 2), lay(g, 1),
                               lay(wa[:, MIX:2 * MIX], 6), lay(wa[:, 3 * MIX:4 * MIX], 6)])
    for l in range(2):
        d[f"w_o{l}"] = lay(x["w_out"][l], KC)
        gu = x["w_gu"][l].reshape(DM, 2, FT, P).transpose(0, 2, 1, 3).reshape(DM, 2 * FF)
        d[f"w_gu{l}"] = lay(gu, 2 * FT)
        for q in range(3):
            k0, k1 = FCUT[q], FCUT[q + 1]
            d[f"w_dn{l}{q}"] = lay(x["w_down"][l][k0 * P:k1 * P], KC, k1 - k0)
    d["w_kv"] = lay(x["w_kv"], 6)
    wb = x["w_in_b"][0]
    d["w_b"] = np.concatenate([lay(wb[:, :MIX], 6), lay(wb[:, MIX + 36:], 2), lay(pad(wb[:, MIX:MIX + 36], P), 1)])
    c = x["state_mlstm_c"][0]
    cut = lambda a, h: (a[:, h, :P], a[:, h, P:]) if h % 2 == 0 else (a[:, h, 64:], a[:, h, :64])

    def order_e(a, h):
        return a if h % 2 == 0 else np.concatenate([a[..., 64:], a[..., :64]], -1)
    d["c_b"] = np.stack([order_e(cut(c, h)[0], h).transpose(1, 0, 2).reshape(P, NB * DH) for h in range(MH)])
    d["c_s"] = np.stack([order_e(cut(c, h)[1], h).transpose(1, 0, 2).reshape(64, NB * DH) for h in range(MH)])
    n = x["state_mlstm_n"][0]
    d["n_b"] = np.stack([cut(n, h)[0].T for h in range(MH)], 1)
    small = [cut(n, h)[1].T for h in range(MH)]
    d["n_s"] = np.concatenate([np.stack(small[0::2], 1), np.stack(small[1::2], 1)], 0)
    d["m0"] = x["state_mlstm_m"][0].T
    mk = x["cache_mem_kv"]
    d["c_mk"] = mk[:, :, :, 0].reshape(2, NB, MEM, 2, P).transpose(0, 4, 1, 3, 2)
    d["c_mv"] = mk[:, :, :, 1].reshape(2, NB, 2, P, MEM).transpose(0, 3, 1, 2, 4)
    d["con2"] = constants2()
    p_ = np.arange(P)
    d["oh"] = np.concatenate([one_hot(p_ - 16 * u - 31) for u in range(-8, 8)] + [one_hot(255 - np.arange(384))], 1)
    d["ohs"] = np.concatenate([one_hot(SEQ - 16 * np.arange(64) - 31), one_hot(P - p_), one_hot(np.zeros(64, int))], 1)
    d["anti"] = np.eye(P, dtype=np.float32)[::-1]
    d["blocks"] = (np.arange(SEQ)[None, :] // 64 == np.arange(16)[:, None]).astype(np.float32)
    d["table"] = x["rel_table"]
    d["table8"] = np.broadcast_to(x["rel_table"][:, None, :], (32, NB, NH))
    d["w1"] = x["cmp_w1"].reshape(2, 16, 2, HD, P).transpose(2, 3, 0, 1, 4).reshape(P, 2, 16, P)
    d["w2"] = x["cmp_w2"].transpose(1, 0, 2)
    d["posT"] = x["cmp_pos"].reshape(16, 2, 2, HD).transpose(1, 3, 2, 0).reshape(P, 2, 16)
    d["b2r"] = np.broadcast_to(x["cmp_b2"][:, None, :], (2, 2, HD)).reshape(1, 256)
    d["gkr"] = np.broadcast_to(x["g_k_cmp"][None, :], (64, HD))
    d["pt"] = x["page_table"].reshape(1, NB * 8)
    d["cmp"] = x["cache_cmp_kv"].reshape(-1, 64, 2, 4, HD).transpose(0, 1, 3, 2, 4).reshape(-1, 64, 512)
    sl = x["cache_slc_kv"].reshape(-1, P, 2, P)
    d["slc"] = np.stack([sl[:, :, 1], sl[:, :, 0].transpose(0, 2, 1)], 2)
    wn = x["cache_win_kv"].reshape(NB, 512, 2, P)
    d["win_k"] = wn[:, :, 0].transpose(0, 2, 1)
    d["win_v"] = wn[:, :, 1].reshape(NB, 4, P, P).transpose(0, 2, 1, 3)
    d["win"] = x["cache_win_kv"].reshape(NB, 512, 256)
    return {k: np.ascontiguousarray(v) for k, v in d.items()}


_OUT = {"o_mem": (8, P, MEM), "o_m": (4, 9), "o_cb": (P, MH, DH + 1), "o_cs": (64, MH, DH + 1),
        "o_scb": (MH, P, NB * DH), "o_scs": (MH, 64, NB * DH), "o_nb": (P, MH, NB), "o_ns": (P, 2, NB),
        "o_kv": (P, 6, N), "o_win": (NB, 512 * 256), "o_y": (P, KC, N)}


def assemble(r):
    def state(cb, cs, h):
        c = np.concatenate([cb, cs] if h % 2 == 0 else [cs, cb], 0)
        return c if h % 2 == 0 else np.concatenate([c[:, P:], c[:, :P]], 1)

    y = r["o_y"].transpose(1, 0, 2).reshape(DM, N).T
    pc = np.stack([state(r["o_cb"][:, h, :DH], r["o_cs"][:, h, :DH], h) for h in range(MH)])[None, None]
    pn = np.stack([np.concatenate([r["o_cb"][:, h, DH], r["o_cs"][:, h, DH]][::1 - 2 * (h % 2)])
                   for h in range(MH)])[None, None]
    mem = r["o_mem"].reshape(2, 2, 4, HD, MEM).transpose(0, 4, 1, 2, 3)[:, None]
    sc = np.stack([[state(r["o_scb"][h].reshape(P, NB, DH)[:, b], r["o_scs"][h].reshape(64, NB, DH)[:, b], h)
                    for h in range(MH)] for b in range(NB)])[None]
    sn = np.stack([[np.concatenate([r["o_nb"][:, h, b], r["o_ns"][64 * (h % 2):64 * (h % 2) + 64, h // 2, b]][::1 - 2 * (h % 2)])
                    for h in range(MH)] for b in range(NB)])[None]
    kv = r["o_kv"].transpose(2, 1, 0).reshape(N, 3, 2, 2, HD)
    win = r["o_win"].reshape(NB, 512, 2, 2, HD)
    out = (y[:SEQ][None], y[SEQ:][:, None], pc, pn, r["o_m"][:, 0][None, None], mem,
           kv[:SEQ, 0][None], kv[:SEQ, 1][None], kv[SEQ - 512:SEQ, 2][None],
           sc, sn, r["o_m"][:, 1:].T[None],
           kv[SEQ:, 0][:, None], kv[SEQ:, 1][:, None], np.concatenate([win[:, 1:], kv[SEQ:, 2][:, None]], 1))
    return tuple(np.ascontiguousarray(a) for a in out)


def kernel(**inputs):
    import concourse.bacc as bacc
    from concourse.bass_utils import run_bass_kernel_spmd

    arrays = lay_inputs({k: np.asarray(v) for k, v in inputs.items()})
    nc = bacc.Bacc("TRN2", target_bir_lowering=False, num_devices=1, dynamic_dma_scratch_size=1024)
    A = {k: nc.dram_tensor(k, v.shape, mybir.dt.from_np(v.dtype), kind="ExternalInput").ap() for k, v in arrays.items()}
    O = {k: nc.dram_tensor(k, s, F32, kind="ExternalOutput").ap() for k, s in _OUT.items()}
    step(nc, A, O)
    r = run_bass_kernel_spmd(nc, [arrays], core_ids=[0])
    return assemble(r.results[0])
```
